# Optimizing a Trainium2 kernel written in Bass

```python
import math
import jax, jax.numpy as jnp
from jax import lax
import numpy as np

D_MODEL = 1024
BATCH = 1
SEQ = 256
DEPTH = 1
DEC_BATCH = 8
DEC_SEQ = 1
PAST_LEN = 2048
PAGE_SIZE = 128

A_HEADS = 8
HEAD_DIM = 64
A_WIDTH = A_HEADS * HEAD_DIM
PATTERNS = ((128, 1), (512, 4), (2048, 16))
MAX_WINDOW = 2048
BLOCK = 128
NUM_BUCKETS = 32
MAX_DISTANCE = 2048
SCALE = HEAD_DIM ** -0.5
NEG = -1e30
R_HEADS = 8
R_HEAD = 64
R_WIDTH = R_HEADS * R_HEAD
DECAY_LORA = 64
AAA_LORA = 64
GATE_LORA = 128
GN_EPS = 64e-5
N_RWKV_COLS = 3 * R_WIDTH + DECAY_LORA + AAA_LORA + GATE_LORA
N_IN_COLS = 3 * A_WIDTH + N_RWKV_COLS + 2 * D_MODEL
N_EXPERTS = 32
TOP_K = 4
D_EXPERT = D_MODEL
SWIGLU_LIMIT = 7.0
SWIGLU_ALPHA = 1.702
MOE_BLOCK = 128
RMS_EPS = 1e-6

kernel_name = 'dilated_rwkv7_moe_hybrid_step'

def rmsnorm(x, g):
    xf = x.astype(jnp.float32)
    y = xf * lax.rsqrt(jnp.mean(xf * xf, axis=-1, keepdims=True) + RMS_EPS)
    return (y * g.astype(jnp.float32)).astype(x.dtype)

def t5_bucket(dist):
    max_exact = NUM_BUCKETS // 2
    d = jnp.maximum(dist, 1).astype(jnp.float32)
    large = max_exact + (jnp.log(d / max_exact) / math.log(MAX_DISTANCE / max_exact)
                         * (NUM_BUCKETS - max_exact)).astype(jnp.int32)
    large = jnp.minimum(large, NUM_BUCKETS - 1)
    return jnp.where(dist < max_exact, dist, large)

def dilated_pattern_prompt(q, k, v, rel_bias, window, dil):
    B, S, H, E = q.shape
    n = window // dil
    assert n <= BLOCK
    sd = -(-S // dil)
    nb = -(-sd // BLOCK)
    s_pad = nb * BLOCK * dil

    def to_blocks(t):
        t = jnp.pad(t, ((0, 0), (0, s_pad - S), (0, 0), (0, 0)))
        t = t.reshape(B, nb * BLOCK, dil, H, E).transpose(0, 2, 1, 3, 4)
        return t.reshape(B, dil, nb, BLOCK, H, E)

    def with_prev(t):
        prev = jnp.pad(t, ((0, 0), (0, 0), (1, 0), (0, 0), (0, 0), (0, 0)))[:, :, :-1]
        return jnp.concatenate([prev, t], axis=3)

    qb = to_blocks(q)
    kb = with_prev(to_blocks(k))
    vb = with_prev(to_blocks(v))
    i = jnp.arange(BLOCK)[:, None]
    j = jnp.arange(2 * BLOCK)[None, :]
    delta = i + BLOCK - j
    band = (delta >= 0) & (delta <= n)
    has_prev = (jnp.arange(nb) > 0)[:, None, None] | (j >= BLOCK)[None]
    mask = band[None] & has_prev
    bias = rel_bias.astype(jnp.float32)[t5_bucket(jnp.clip(delta, 0, n) * dil)].transpose(2, 0, 1)
    s = jnp.einsum('brcihe,brcjhe->brchij', qb, kb) * SCALE + bias[None, None, None]
    s = jnp.where(mask[None, None, :, None], s, NEG)
    m = jnp.max(s, axis=-1, keepdims=True)
    p = jnp.exp(s - m)
    l = jnp.sum(p, axis=-1, keepdims=True)
    o = jnp.einsum('brchij,brcjhe->brcihe', p / l, vb)
    lse = jnp.swapaxes((m + jnp.log(l))[..., 0], 3, 4)
    o = o.reshape(B, dil, nb * BLOCK, H, E).transpose(0, 2, 1, 3, 4).reshape(B, s_pad, H, E)[:, :S]
    lse = lse.reshape(B, dil, nb * BLOCK, H).transpose(0, 2, 1, 3).reshape(B, s_pad, H)[:, :S]
    return o, lse

def merge_patterns(outs, lses):
    wts = jax.nn.softmax(jnp.stack(lses, 0), axis=0)
    return jnp.einsum('gbth,gbthe->bthe', wts, jnp.stack(outs, 0))

def dilated_attn_prompt(q, k, v, rel_bias):
    q, k, v = (t.astype(jnp.float32) for t in (q, k, v))
    res = [dilated_pattern_prompt(q, k, v, rel_bias, w, d) for (w, d) in PATTERNS]
    return merge_patterns([r[0] for r in res], [r[1] for r in res])

def dilated_attn_sample(q, k_new, v_new, cache_k, cache_v, rel_bias):
    wb = cache_k.shape[1]
    L = q.shape[1]
    q = q.astype(jnp.float32)
    kc = jnp.concatenate([cache_k.astype(jnp.float32), k_new.astype(jnp.float32)], axis=1)
    vc = jnp.concatenate([cache_v.astype(jnp.float32), v_new.astype(jnp.float32)], axis=1)
    outs, lses = [], []
    for (window, dil) in PATTERNS:
        n = window // dil
        jj = jnp.arange(n + 1)
        idx = wb + jnp.arange(L)[:, None] - jj[None, :] * dil
        valid = idx >= 0
        idx = jnp.maximum(idx, 0)
        kg = kc[:, idx]
        vg = vc[:, idx]
        bias = rel_bias.astype(jnp.float32)[t5_bucket(jj * dil)]
        s = jnp.einsum('blhe,bljhe->bhlj', q, kg) * SCALE + bias.T[None, :, None, :]
        s = jnp.where(valid[None, None], s, NEG)
        lse = jax.nn.logsumexp(s, axis=-1)
        p = jnp.exp(s - lse[..., None])
        outs.append(jnp.einsum('bhlj,bljhe->blhe', p, vg))
        lses.append(lse.transpose(0, 2, 1))
    return merge_patterns(outs, lses)

def rwkv_scan(S0, r, decay, k, v, kk, a):
    def step(S, inp):
        r_t, w_t, k_t, v_t, kk_t, a_t = inp
        sa = jnp.einsum('bhvk,bhk->bhv', S, -kk_t)
        S = (S * w_t[:, :, None, :] + sa[..., None] * (kk_t * a_t)[:, :, None, :]
             + v_t[..., None] * k_t[:, :, None, :])
        return S, jnp.einsum('bhvk,bhk->bhv', S, r_t)
    xs = tuple(t.transpose(1, 0, 2, 3) for t in (r, decay, k, v, kk, a))
    S, ys = lax.scan(step, S0, xs)
    return S, ys.transpose(1, 0, 2, 3)

def moe(h, w_router, b_router, w_gate_up, b_gate_up, w_down, b_down):
    B, T, D = h.shape
    xt = h.reshape(-1, D)
    N = xt.shape[0]
    logits = (xt @ w_router + b_router).astype(jnp.float32)
    top_v, top_i = lax.top_k(logits, TOP_K)
    gate = jax.nn.softmax(top_v, axis=-1)
    nk = N * TOP_K
    e_flat = top_i.reshape(-1)
    tok_flat = jnp.repeat(jnp.arange(N, dtype=jnp.int32), TOP_K)
    g_flat = gate.reshape(-1)
    order = jnp.argsort(e_flat)
    e_s, tok_s, g_s = e_flat[order], tok_flat[order], g_flat[order]
    sizes = jnp.bincount(e_flat, length=N_EXPERTS)
    starts = jnp.cumsum(sizes) - sizes
    padded = (sizes + MOE_BLOCK - 1) // MOE_BLOCK * MOE_BLOCK
    pends = jnp.cumsum(padded)
    pstarts = pends - padded
    dest = pstarts[e_s] + jnp.arange(nk) - starts[e_s]
    n_slots = -(-(nk + N_EXPERTS * (MOE_BLOCK - 1)) // MOE_BLOCK) * MOE_BLOCK
    n_blocks = n_slots // MOE_BLOCK
    slot_tok = jnp.full((n_slots,), N, jnp.int32).at[dest].set(tok_s)
    slot_gate = jnp.zeros((n_slots,), jnp.float32).at[dest].set(g_s)
    block_e = jnp.minimum(jnp.searchsorted(pends, jnp.arange(n_blocks) * MOE_BLOCK, side='right'), N_EXPERTS - 1)
    xpad = jnp.concatenate([xt, jnp.zeros((1, D), xt.dtype)], axis=0)
    xs = xpad[slot_tok].reshape(n_blocks, MOE_BLOCK, D)

    def expert_block(args):
        xb, e = args
        gu = xb @ w_gate_up[e] + b_gate_up[e]
        gt, up = gu[..., :D_EXPERT], gu[..., D_EXPERT:]
        gt = jnp.minimum(gt, SWIGLU_LIMIT)
        up = jnp.clip(up, -SWIGLU_LIMIT, SWIGLU_LIMIT)
        act = (up + 1) * (gt * jax.nn.sigmoid(gt * SWIGLU_ALPHA))
        return act @ w_down[e] + b_down[e]

    ys = lax.map(expert_block, (xs, block_e)).reshape(n_slots, D)
    out = jnp.zeros((N + 1, D), jnp.float32).at[slot_tok].add(ys.astype(jnp.float32) * slot_gate[:, None])[:N]
    return out.reshape(B, T, D).astype(h.dtype)

def hybrid_layer(x, shift_prev, wkv0, attend, ln1, w_in, rwkv_mu, w0, w_decay_up, a0, w_a_up, w_g_up,
                 k_k, k_a, r_k, gn_w, gn_b, w_branch_a, w_branch_b, w_out, ln2,
                 w_router, b_router, w_gate_up, b_gate_up, w_down, b_down):
    B, T, _ = x.shape
    f32 = jnp.float32
    h = rmsnorm(x, ln1)
    proj = h @ w_in
    c1 = 3 * A_WIDTH
    c2 = c1 + N_RWKV_COLS
    qkv = proj[..., :c1].reshape(B, T, 3, A_HEADS, HEAD_DIM)
    q, k, v = qkv[:, :, 0], qkv[:, :, 1], qkv[:, :, 2]
    rc = proj[..., c1:c2]
    gates = proj[..., c2:]
    o_a = attend(q, k, v)
    prev = jnp.concatenate([shift_prev[:, None].astype(rc.dtype), rc[:, :-1]], axis=1)
    xr = (rc + (prev - rc) * rwkv_mu).astype(f32)
    r, kr, vr, xw, xa, xg = jnp.split(
        xr, [R_WIDTH, 2 * R_WIDTH, 3 * R_WIDTH, 3 * R_WIDTH + DECAY_LORA, 3 * R_WIDTH + DECAY_LORA + AAA_LORA], axis=-1)
    wlog = -jax.nn.softplus(-(w0 + jnp.tanh(xw) @ w_decay_up)) - 0.5
    decay = jnp.exp(-jnp.exp(wlog))
    a = jax.nn.sigmoid(a0 + xa @ w_a_up)
    g = jax.nn.sigmoid(xg) @ w_g_up
    kk = kr * k_k
    kr = kr * (1 + (a - 1) * k_a)
    heads = lambda t: t.reshape(B, T, R_HEADS, R_HEAD)
    kk = heads(kk)
    kk = kk / jnp.maximum(jnp.sqrt(jnp.sum(kk * kk, axis=-1, keepdims=True)), 1e-12)
    rh, kh, vh = heads(r), heads(kr), heads(vr)
    wkv_T, y = rwkv_scan(wkv0.astype(f32), rh, heads(decay), kh, vh, kk, heads(a))
    mu = jnp.mean(y, axis=-1, keepdims=True)
    var = jnp.mean(jnp.square(y - mu), axis=-1, keepdims=True)
    yn = ((y - mu) * lax.rsqrt(var + GN_EPS)).reshape(B, T, R_WIDTH) * gn_w + gn_b
    bonus = (jnp.sum(rh * kh * r_k, axis=-1, keepdims=True) * vh).reshape(B, T, R_WIDTH)
    o_b = (yn + bonus) * g
    gate_a, gate_b = jnp.split(gates, 2, axis=-1)
    mixed = (jax.nn.sigmoid(gate_a) * (o_a.reshape(B, T, A_WIDTH).astype(x.dtype) @ w_branch_a)
             + jax.nn.sigmoid(gate_b) * (o_b.astype(x.dtype) @ w_branch_b))
    x = x + mixed @ w_out
    x = x + moe(rmsnorm(x, ln2), w_router, b_router, w_gate_up, b_gate_up, w_down, b_down)
    return x, k, v, wkv_T, rc[:, -1]

def setup_inputs(seed: int = 0) -> dict:
    key = jax.random.key(seed)
    ks = iter(jax.random.split(key, 40))
    nrm = lambda shape, scale: jax.random.normal(next(ks), shape, jnp.float32) * scale
    wbuf = min(MAX_WINDOW, PAST_LEN)
    L = DEPTH
    return {
        'x_prompt': nrm((BATCH, SEQ, D_MODEL), 1.0),
        'x_sample': nrm((DEC_BATCH, DEC_SEQ, D_MODEL), 1.0),
        'cache_k': nrm((L, DEC_BATCH, wbuf, A_HEADS, HEAD_DIM), 1.0),
        'cache_v': nrm((L, DEC_BATCH, wbuf, A_HEADS, HEAD_DIM), 1.0),
        'state_wkv': nrm((L, DEC_BATCH, R_HEADS, R_HEAD, R_HEAD), 0.3),
        'state_shift': nrm((L, DEC_BATCH, N_RWKV_COLS), 1.0),
        'rel_bias': nrm((NUM_BUCKETS, A_HEADS), 0.3),
        'ln1': 1.0 + nrm((L, D_MODEL), 0.01),
        'w_in': nrm((L, D_MODEL, N_IN_COLS), D_MODEL ** -0.5),
        'rwkv_mu': jax.random.uniform(next(ks), (L, N_RWKV_COLS), jnp.float32),
        'w0': jax.random.uniform(next(ks), (L, R_WIDTH), jnp.float32, -4.0, 1.0),
        'w_decay_up': nrm((L, DECAY_LORA, R_WIDTH), 0.5 * DECAY_LORA ** -0.5),
        'a0': nrm((L, R_WIDTH), 0.1),
        'w_a_up': nrm((L, AAA_LORA, R_WIDTH), AAA_LORA ** -0.5),
        'w_g_up': nrm((L, GATE_LORA, R_WIDTH), GATE_LORA ** -0.5),
        'k_k': 0.85 + nrm((L, R_WIDTH), 0.05),
        'k_a': 1.0 + nrm((L, R_WIDTH), 0.05),
        'r_k': nrm((L, R_HEADS, R_HEAD), 0.1),
        'gn_w': 1.0 + nrm((L, R_WIDTH), 0.01),
        'gn_b': nrm((L, R_WIDTH), 0.01),
        'w_branch_a': nrm((L, A_WIDTH, D_MODEL), A_WIDTH ** -0.5),
        'w_branch_b': nrm((L, R_WIDTH, D_MODEL), R_WIDTH ** -0.5),
        'w_out': nrm((L, D_MODEL, D_MODEL), D_MODEL ** -0.5),
        'ln2': 1.0 + nrm((L, D_MODEL), 0.01),
        'w_router': nrm((L, D_MODEL, N_EXPERTS), D_MODEL ** -0.5),
        'b_router': nrm((L, N_EXPERTS), 0.01),
        'w_gate_up': nrm((L, N_EXPERTS, D_MODEL, 2 * D_EXPERT), D_MODEL ** -0.5),
        'b_gate_up': nrm((L, N_EXPERTS, 2 * D_EXPERT), 0.01),
        'w_down': nrm((L, N_EXPERTS, D_EXPERT, D_MODEL), D_EXPERT ** -0.5),
        'b_down': nrm((L, N_EXPERTS, D_MODEL), 0.01),
        'ln_f': 1.0 + nrm((D_MODEL,), 0.01),
    }

def reference(x_prompt, x_sample, cache_k, cache_v, state_wkv, state_shift, rel_bias, ln1, w_in, rwkv_mu,
              w0, w_decay_up, a0, w_a_up, w_g_up, k_k, k_a, r_k, gn_w, gn_b, w_branch_a, w_branch_b, w_out,
              ln2, w_router, b_router, w_gate_up, b_gate_up, w_down, b_down, ln_f):
    xp, xs = x_prompt, x_sample
    Bp = xp.shape[0]
    wp = min(MAX_WINDOW, xp.shape[1])
    pk, pv, pwkv, psh, sk, sv, swkv, ssh = [], [], [], [], [], [], [], []
    for l in range(DEPTH):
        lw = (ln1[l], w_in[l], rwkv_mu[l], w0[l], w_decay_up[l], a0[l], w_a_up[l], w_g_up[l], k_k[l], k_a[l],
              r_k[l], gn_w[l], gn_b[l], w_branch_a[l], w_branch_b[l], w_out[l], ln2[l], w_router[l], b_router[l],
              w_gate_up[l], b_gate_up[l], w_down[l], b_down[l])
        xp, kp_, vp_, wkvp_, shp_ = hybrid_layer(
            xp, jnp.zeros((Bp, N_RWKV_COLS), xp.dtype), jnp.zeros((Bp, R_HEADS, R_HEAD, R_HEAD), jnp.float32),
            lambda q, k, v: dilated_attn_prompt(q, k, v, rel_bias), *lw)
        xs, ks_, vs_, wkvs_, shs_ = hybrid_layer(
            xs, state_shift[l], state_wkv[l],
            lambda q, k, v, l=l: dilated_attn_sample(q, k, v, cache_k[l], cache_v[l], rel_bias), *lw)
        pk.append(kp_[:, -wp:])
        pv.append(vp_[:, -wp:])
        pwkv.append(wkvp_)
        psh.append(shp_)
        sk.append(ks_)
        sv.append(vs_)
        swkv.append(wkvs_)
        ssh.append(shs_)
    y_prompt = rmsnorm(xp, ln_f)
    y_sample = rmsnorm(xs, ln_f)
    return (y_prompt, y_sample, jnp.stack(pk, 0), jnp.stack(pv, 0), jnp.stack(pwkv, 0), jnp.stack(psh, 0),
            jnp.stack(sk, 0), jnp.stack(sv, 0), jnp.stack(swkv, 0), jnp.stack(ssh, 0))


_drawn_inputs = setup_inputs


def setup_inputs(seed=0):
    import zlib

    import numpy as np

    out = dict(_drawn_inputs(seed))
    spreads = {}
    factors = {'ln1': 2.77,
     'gn_w': 21.521,
     'gn_b': 36.812,
     'b_gate_up': 23.156,
     'b_down': 64.0,
     'ln_f': 166.049,
     'ln2': 4.089,
     'b_router': 4.273}
    for name, (base, spread) in spreads.items():
        noise = np.random.default_rng([zlib.crc32(name.encode()), seed]).standard_normal(out[name].shape)
        drawn = base * np.exp(spread * noise) if base else spread * noise
        out[name] = __import__('jax').numpy.asarray(drawn.astype(out[name].dtype))
    for name, factor in factors.items():
        out[name] = (out[name] * factor).astype(out[name].dtype)
    return out
```

```python
import concourse.bass as bass
from concourse import mybir
from contextlib import ExitStack
import numpy as np

F32 = mybir.dt.float32
I32 = mybir.dt.int32
ALU = mybir.AluOpType
ACT = mybir.ActivationFunctionType
AX = mybir.AxisListType

D = 1024
S = 256
NB = 8
T = S + NB
ROWS = [128, 128, NB]
NM = len(ROWS)
KD = D // 128
H = 8
E64 = 64
PAST = 2048
CA, CR, CG = 12, 14, 16
NPROJ = CA + CR + CG
NIN = NPROJ * 128
RC = CR * 128
SCALE = E64 ** -0.5
DECAY = float(np.exp(-0.5))
CH = 32
NCH = S // CH
NE = 32
FE = 1024
SLOT = 64
PASSES = -(-T // SLOT)
LIMIT, ALPHA = 7.0, 1.702
NEG = -1e30
BIG = 3e38
NREL = 383
KT = [128, 96, 97]
KO = [0, 128, 224]
NKEY = 321

P_LN1, P_MU, P_W0, P_A0, P_KK, P_KA, P_RK, P_GW, P_GB, P_N = 0, 8, 22, 26, 30, 34, 38, 42, 46, 50
CONST_NAMES = ["ident", "ones", "head_sum", "head_mean", "lo8", "up8", "up16", "up32", "strict", "incl",
               "neg_incl", "before", "slots", "idstack", "quad"]


def shape_constants():
    p = np.arange(128)[:, None]
    c = np.arange(128)[None, :]
    same = lambda n: p // n == c // n
    m = {
        "ident": p == c, "ones": p >= 0 * c, "head_sum": same(64), "head_mean": same(64) / 64.0,
        "lo8": same(8) & (c < p), "up8": same(8) & (p < c), "up16": same(16) & ~same(8) & (p < c),
        "up32": same(32) & ~same(16) & (p < c), "strict": same(32) & (p < c), "incl": same(32) & (p <= c),
        "neg_incl": -1.0 * (same(32) & (p <= c)), "before": p < c, "slots": 0 * p + c % SLOT + 1,
        "idstack": (p % 64 == c) & (c < 64), "quad": (p // 32 == c) & (c < 4),
    }
    mats = np.concatenate([(np.ones((128, 128)) * m[n]).astype(np.float32) for n in CONST_NAMES], axis=1)

    def bucket(d):
        d = np.asarray(d)
        f = np.maximum(d, 1).astype(np.float32)
        large = 16 + (np.log(f / np.float32(16)) / np.float32(np.log(2048 / 16)) * np.float32(16)).astype(np.int32)
        return np.where(d < 16, d, np.minimum(large, 31))

    def count(d):
        return (1 * (d <= 128) + 1 * ((d % 4 == 0) & (d <= 512)) + 1 * ((d % 16 == 0) & (d <= 2048))) * (d >= 0)

    dist_p = 255 - np.arange(NREL)
    dist_s = np.concatenate([128 - np.arange(128), 512 - 4 * np.arange(96), 2048 - 16 * np.arange(96), [0]])
    out = []
    for dist, rows in ((dist_p, H), (dist_s, NB * H)):
        hot = (np.arange(32)[:, None] == bucket(np.maximum(dist, 0))[None, :]).astype(np.float32)
        n = count(dist)
        log = np.where(n > 0, np.log(np.maximum(n, 1).astype(np.float32)), np.float32(NEG)).astype(np.float32)
        out += [hot, np.ascontiguousarray(np.broadcast_to(log, (rows, len(dist))))]
    return {"c_mats": mats, "c_hot_p": out[0], "c_log_p": out[1], "c_hot_s": out[2], "c_log_s": out[3],
            "c_own": (np.arange(128)[:, None] % 32 == np.arange(512)[None, :] // 64).astype(np.float32)}


def psum_jobs():
    jobs = ["par", "ssT"] + [f"hT{m}{g}" for m in range(NM) for g in range(2)]
    pr = lambda *groups: [f"pr{g * GC + j}" for g in groups for j in range(GC)]
    jobs += pr(2, 3, 4) + ["bvp", "bvs"] + [f"sh{g}" for g in range(4)] + pr(0)
    jobs += [f"lw{c}" for c in range(4)] + [f"la{c}" for c in range(4)] + [f"lg{c}" for c in range(4)] + pr(1)
    jobs += [f"nk{c}" for c in range(4)] + pr(5, 6)
    jobs += ["qn"] + [f"kn{m}" for m in range(NM)] + [f"vn{m}" for m in range(NM)]
    jobs += ["s0", "s1"]
    jobs += [x for h in range(H) for x in ([f"s{h + 2}"] * (h + 2 < H) + [f"pt{h}"] + [f"ov{h // 2}"] * (h % 2))]
    jobs += ["sst", "spt", "pv0", "pv1", "sv"] + [f"sx{v}" for v in range(6)]
    jobs += [f"bo{c}" for c in range(4)]
    jobs += [f"{k}{m}" for m in range(2) for k in ("tV", "tK", "tC", "tB")]
    grp = [(m, par) for m in range(2) for par in range(2)]
    for k in ("Auk", "Brk", "Aub", "Brb", "A8", "A2", "A2T", "X1T", "A4", "X", "XT", "LX", "X2", "X2T", "LX2",
              "MT", "AV", "HG", "Y0", "Rp"):
        jobs += [f"{k}{m}{par}" for m, par in grp]
    jobs += [f"TZ{c}" for c in range(NCH)]
    jobs += [f"st{c}" for c in range(1, NCH)]
    jobs += [f"yt{c}" for c in range(1, NCH)] + ["wkv", "sy"]
    jobs += [f"mu{c}" for c in range(4)] + [f"va{c}" for c in range(4)]
    jobs += [x for d in range(KD) for x in (f"ma{d}", f"mb{d}")]
    jobs += [f"wo{m}{g}" for m in range(NM) for g in range(2)]
    jobs += [f"ht{m}{g}" for m in range(NM) for g in range(2)]
    jobs += ["lg", "rk", "gT"] + [f"bd{m}{g}" for m in range(NM) for g in range(2)]
    return jobs


CMB = [(0, 1), (6, 7), (4, 5)]
GROUPS = [2, 3, 4, 0, 1, 5, 6]
GC = 6


def proj_order():
    return [g * GC + j for g in GROUPS for j in range(GC)]


def build(nc, A, O):
    jobs = psum_jobs()
    assert len(set(jobs)) == len(jobs)
    bank = {j: n % 8 for n, j in enumerate(jobs)}
    turn = {j: n // 8 + 1 for n, j in enumerate(jobs)}

    with ExitStack() as ctx:
        def sb(name, n, dt=F32, parts=128):
            return ctx.enter_context(nc.sbuf_tensor(name, [parts, n], dt))

        def sem(name):
            return ctx.enter_context(nc.semaphore(name))

        RING = sb("ring", 24576)
        WORK = sb("work", 28600)
        PS = [ctx.enter_context(nc.psum_tensor(f"ps{b}", [128, 512], F32)) for b in range(8)]

        def view(base, off, *dims):
            n = int(np.prod(dims))
            v = base[:, off:off + n]
            if len(dims) > 1:
                names = "abcd"[:len(dims)]
                v = v.rearrange("p (" + " ".join(names) + ") -> p " + " ".join(names),
                                **{k: d for k, d in zip(names[1:], dims[1:])})
            return v

        def bc(ap, at, n):
            ap = ap.unsqueeze(at)
            shape = list(ap.shape)
            shape[at] = n
            return ap.broadcast_to(shape)

        mats = view(WORK, 0, len(CONST_NAMES), 128)
        C = {n: mats[:, i, :] for i, n in enumerate(CONST_NAMES)}
        sm = [128 * len(CONST_NAMES)]

        def small(*dims):
            v = view(WORK, sm[0], *dims)
            sm[0] += int(np.prod(dims))
            assert sm[0] <= 2792
            return v

        par = small(128)
        parT = small(P_N)
        ssT = small(CR, NB)
        sq1 = small(3)
        rs1 = small(3)
        eps = small(1)
        sgs = small(4, NB)
        pcs = small(4, NCH)
        relb = small(H)
        relb64 = small(NB, H)
        sqs = small(4, NB)
        svT = small(6, 4, NB)
        negm = small(H, 2)
        lsum = small(H, 2)
        rinv = small(H, 2)
        nms = small(1)
        lss = small(1)
        ris = small(1)
        ysm = small(2, 16)
        mcount = small(1)
        thr = small(PASSES)
        qkvT = view(WORK, 2792, CA, T)
        sgT = view(WORK, 5960, CG, T)
        rcT = view(WORK, 10184, CR, T)
        xr = view(WORK, 13880, CR, T)
        hT = view(WORK, 17576, KD, T)
        oaT = view(WORK, 19688, 4, T)
        wlora = view(WORK, 19688, 2, 512)
        e = [view(WORK, 20744 + 1024 * i, 4, S) for i in range(6)]
        kkn = view(WORK, 20744 + 6144, 4, T)
        spare = 20744 + 6144 + 1056
        ysn = view(WORK, spare, 512)
        aT = view(WORK, 10184, 4, T)
        gT_ = view(WORK, 10184 + 1056, 4, T)
        bT = view(WORK, 10184 + 2112, 4, T)
        scanX = view(WORK, 20744 + 4096, 4 * NCH, 2 * CH)
        Y0 = view(WORK, 17576, 4, S)
        Rp = view(WORK, 17576 + 1024, 4, S)
        svn = view(WORK, 2792, 6, 512)
        S1 = view(WORK, 2792, 16, E64)
        S1t = view(WORK, 2792 + 1024, 16, E64)
        svec = view(WORK, 2792 + 2048, 6, E64)
        u1 = view(WORK, 2792 + 2048 + 384, 16)
        mixT = view(WORK, 17576, KD, T)
        WIN = [view(RING, 6144 * i, KD, GC * 128) for i in range(2)]
        qB = view(RING, 0, NB, 512)
        kn = view(RING, 4096, NM, 512)
        vn = view(RING, 5632, NM, 512)
        ssb = view(RING, 7168, 2, 384)
        ptb = view(RING, 7936, 2, 384)
        PROD = [view(RING, 8704 + 1536 * i, 3, 512) for i in range(2)]
        qn = view(RING, 11776, 512)
        own = view(RING, 11776, 512)
        B3 = view(RING, 12288, H, 384)
        shn = view(RING, 15360, RC)
        scanY = view(RING, 15360, 4 * NCH, 2 * CH)
        pts = view(RING, 15360, 3, NB, 32)
        pvm = view(RING, 15360 + 768, 2, 512)
        biasS = view(RING, 17408, NKEY)
        s64 = view(RING, 17729, NKEY)
        scs = view(RING, 18050, 3, 64)
        X = view(RING, 18432, NM, D)
        XS = view(RING, 18432 + 3072, NM, D)
        bvec = view(WORK, spare, NREL)
        ss = view(WORK, 20744, RC)
        Kb = [view(RING, 18432 + 1536 * i, 3, 512) for i in range(2)]
        Vb = [view(RING, 18432 + 3072 + 1536 * i, 3, 512) for i in range(2)] + Kb
        hot_p = view(WORK, 20744 + 1792, NREL)
        log_p = view(WORK, 20744 + 1792 + 383, NREL)
        hot_s = view(WORK, 20744 + 1792 + 766, NKEY)
        log_s = view(WORK, 20744 + 1792 + 766 + 321, NKEY)
        arr = [view(RING, 2048 * i, 4, 4, 128) for i in range(10)]
        natV = view(RING, 20480, 2, 512)
        natK = view(RING, 20480 + 1024, 2, 512)
        natC = view(RING, 20480 + 2048, 2, 512)
        natB = view(RING, 20480 + 3072, 2, 512)
        aA, aAT, aL1T, aL2T, aBrk, aBrb, aAuk, aA2, aA2T, aI = arr
        HG = aA2
        AV = view(RING, 2048 * 2, 4, 4, 64)
        TT = view(RING, 0, NCH, 4, 128)
        Zc = view(RING, 2048 * 2, NCH, 4, 64)
        STd = view(RING, 2048 * 3, 4, 4, 128)
        STe = view(RING, 2048 * 9, 4, 4, 128)
        stc = [view(RING, 2048 * 6 + 256 * i, 4, 64) for i in range(NCH + 1)]
        del stc
        stc = [view(RING, 2048 * 6 + 256 * i, 4, 64) for i in range(NCH)]
        wkvn = view(WORK, 20744 + 3072, 4, 128)
        wa = view(RING, 2048 * 4, 4, D)
        wb = view(RING, 2048 * 7, 4, D)
        wo = view(RING, 0, KD, D)

        YT = view(WORK, 20744 + 6144, 4, T)
        e4w = view(WORK, 20744 + 4096, 4, T)
        dtmp = view(WORK, 20744 + 1024, 4, 64)
        UNIT = [view(RING, 2048 * u, 2048) for u in (6, 9, 10, 11, 4, 5, 7, 8, 0, 1, 2, 3)]
        acc = view(WORK, 2792, NM, D)
        brow = view(WORK, 5960, 2 * FE)
        wr = view(WORK, 8008, KD, NE)
        bdn = view(WORK, 8264, D)
        brow_r = view(WORK, 9288, NE)
        gateT = view(WORK, 9320, NM, 128)
        h2 = view(WORK, 10184, NM, D)
        ln2b = view(WORK, 13880, D)
        lnfb = view(WORK, 13880 + 1024, D)
        h2T = view(WORK, 17576, KD, T)
        mo = [19688]

        def moe_small(*dims):
            t = view(WORK, mo[0], *dims)
            mo[0] += int(np.prod(dims))
            return t

        posx = moe_small(NM, PASSES * NE + 1)
        gate = moe_small(NM, NE)
        selr = moe_small(NM, NE)
        lgt = moe_small(NM, NE + 4)
        rep = moe_small(NM, NE + 4)
        max8 = moe_small(NM, 8)
        ngm = moe_small(NM)
        gsum = moe_small(NM)
        assert mo[0] <= 20744
        mo[0] = 20744
        rexp = moe_small(NM, NE)
        sel = moe_small(NM, SLOT)
        selg = moe_small(NM, 128)
        xg = moe_small(512)
        xgT = moe_small(4, 128)
        gt = moe_small(512)
        up = moe_small(512)
        sg = moe_small(512)
        actT = moe_small(4, 128)
        yS = moe_small(512)
        selgT = moe_small(384)
        npass = sb("npass", 1, I32)
        full = [sem(f"bank{b}_full") for b in range(8)]
        evac = [sem(f"bank{b}_evacuated") for b in range(8)]
        SEM = {}

        def S_(name):
            if name not in SEM:
                SEM[name] = sem(name)
            return SEM[name]

        def take(eng, job):
            eng.wait_ge(full[bank[job]], turn[job])

        def after(eng, *names):
            for job in names:
                eng.wait_ge(evac[bank[job]], turn[job])

        def psum(job, *dims, parts=128):
            return view(PS[bank[job]], 0, *dims)[:parts]

        class Chain:

            def __init__(self, eng, name):
                self.eng, self.sem, self.n = eng, S_(name), 0

            def __call__(self, ins):
                self.n += 1
                ins.then_inc(self.sem, 1)
                self.eng.wait_ge(self.sem, self.n)

            def free(self, ins, job):
                ins.then_inc(evac[bank[job]], 1)
                self.eng.wait_ge(evac[bank[job]], turn[job])

            def ready(self, ins, name, n=1):
                ins.then_inc(S_(name), 1)
                self.eng.wait_ge(S_(name), n)

        GRP = [(m, par_) for m in range(2) for par_ in range(2)]
        bvec_d = nc.dram_tensor("bias_rows", (H, 128, NREL), F32, kind="Internal").ap()
        qn_d = nc.dram_tensor("sample_q", (NB, 512), F32, kind="Internal").ap()
        sv_d = nc.dram_tensor("sample_vectors", (NB, 6, 512), F32, kind="Internal").ap()
        ys_d = nc.dram_tensor("sample_y", (2, NB * H, 32), F32, kind="Internal").ap()
        block = ctx.enter_context(nc.Block())

        LOADS = {"ld_x": 3, "ld_mats": 1, "ld_par": 9, "ld_ss": 1, "ld_lora": 3, "ld_bias": 6}

        @block.sync
        def _(sp):
            def load(dst, src, name):
                sp.dma_start(dst, src).then_inc(S_(name), 16)

            def wait_pe(job):
                sp.wait_ge(full[bank[job]], turn[job])

            for m in range(2):
                load(X[:, m, :], A["x_prompt"][0, m * 128:(m + 1) * 128, :], "ld_x")
            load(X[:NB, 2, :], A["x_sample"][:, 0, :], "ld_x")
            load(WORK[:, 0:128 * len(CONST_NAMES)], A["c_mats"], "ld_mats")

            def load_win(i):
                g = GROUPS[i]
                src = A["w_in"][0, :, g * 768:(g + 1) * 768].rearrange("(k p) n -> p k n", p=128)
                load(WIN[i % 2], src, f"ld_win{i}")

            sp.wait_ge(S_("ld_par"), 16 * 9)
            sp.wait_ge(S_("ld_ss"), 16)
            for i in range(2):
                load_win(i)
            for i in range(2, 7):
                wait_pe(f"pr{GROUPS[i - 2] * GC + GC - 1}")
                load_win(i)
            cuts = ((0, 128, 1920, 1), (1, 96, 1536, 4), (2, 96, 0, 16))

            def load_cache(dst, src, b, new, name):
                for t, n, first, step in cuts:
                    rows = src[0, b, first:first + step * (n - 1) + 1:step].rearrange("s h d -> s (h d)")
                    load(dst[:n, t, :], rows, name)
                load(dst[96:97, 2, :], new[b:b + 1, 2, :], name)

            sp.wait_ge(S_("kv_zero"), 1)
            after(sp, "kn2")
            for b in range(NB):
                if b >= 2:
                    sp.wait_ge(S_("pool_prod"), b - 1)
                load_cache(Kb[b % 2], A["cache_k"], b, kn, f"ld_k{b % 2}")
                if b == 1:
                    after(sp, "vn2")
                    for v in range(2):
                        load_cache(Vb[v], A["cache_v"], v, vn, f"ld_v{v}")
            for b in range(2, 4):
                sp.wait_ge(S_("pool_prod"), 5 + b)
                load_cache(Vb[b], A["cache_v"], b, vn, f"ld_v{b}")
            wait_pe("pv0")
            for b in range(4):
                load_cache(Vb[b], A["cache_v"], 4 + b, vn, f"ld_v{b}")
            wait_pe("Rp11")
            load(wa, A["w_branch_a"][0].rearrange("(k p) n -> p k n", p=128), "ld_wa")
            wait_pe("TZ7")
            load(wb, A["w_branch_b"][0].rearrange("(k p) n -> p k n", p=128), "ld_wb")
            after(sp, "yt7")
            load(wo, A["w_out"][0].rearrange("(k p) n -> p k n", p=128), "ld_wo")
            sp.wait_ge(S_("ld_ysn"), 16)
            for m in range(2):
                load(acc[:, m, :], A["x_prompt"][0, m * 128:(m + 1) * 128, :], "ld_acc")
            load(acc[:NB, 2, :], A["x_sample"][:, 0, :], "ld_acc")
            sp.wait_ge(S_("obT"), 1)
            load(ln2b, A["ln2"].broadcast_to([128, D]), "ld_ln")
            load(lnfb, A["ln_f"].unsqueeze(0).broadcast_to([128, D]), "ld_ln")
            sp.wait_ge(S_("mix"), KD)
            load(wr, A["w_router"][0].rearrange("(k p) e -> p k e", p=128), "ld_router")
            load(brow_r, A["b_router"].broadcast_to([128, NE]), "ld_router")
            load(bdn[:NE], A["b_down"][0], "ld_router")
            wgu = A["w_gate_up"][0]
            wdn = A["w_down"][0]

            def load_expert(ex, free):
                for k in range(KD):
                    free(k + 1)
                    sp.dma_start(UNIT[k], wgu[bass.ds(ex, 1), k * 128:(k + 1) * 128, :].rearrange("a p n -> p (a n)")).then_inc(S_(f"ld_u{k}"), 16)
                for u in range(4):
                    free(KD + u + 1)
                    sp.dma_start(UNIT[KD + u].rearrange("p (j n) -> p j n", j=2),
                                 wdn[bass.ds(ex, 1), u * 256:(u + 1) * 256, :].rearrange("a (j p) n -> p (a j) n", p=128))\
                      .then_inc(S_(f"ld_u{KD + u}"), 16)
                    if u == 0:
                        sp.wait_ge(S_("brow_zero"), 1)
                        sp.dma_start(brow[0:1, :], A["b_gate_up"][0, bass.ds(ex, 1), :]).then_inc(S_("ld_b"), 16)

            load_expert(0, lambda n: sp.wait_ge(S_("unit_used"), n))
            with sp.Fori(1, NE) as ex:
                load_expert(ex, lambda n: sp.wait_ge(S_("unit_used"), ex * 12 + n))
            sp.wait_ge(S_("npass"), 1)
            passes = sp.value_load(npass[0:1, 0:1], min_val=1, max_val=PASSES)
            with sp.If(passes > 1):
                with sp.Fori(1, passes) as p:
                    with sp.Fori(0, NE) as ex:
                        it = sp.snap(p * NE + ex)
                        load_expert(ex, lambda n: sp.wait_ge(S_("unit_used"), it * 12 + n))
            sp.wait_ge(S_("acc_final"), 1)

        @block.scalar
        def _(act):
            A_ = Chain(act, "act_step")

            def load(dst, src, name):
                act.dma_start(dst, src).then_inc(S_(name), 16)

            row = lambda name, n: A[name].rearrange("l (c p) -> (l c) p", p=128)
            for name, at, n in (("ln1", P_LN1, 8), ("rwkv_mu", P_MU, CR), ("w0", P_W0, 4), ("a0", P_A0, 4),
                                ("k_k", P_KK, 4), ("k_a", P_KA, 4), ("gn_w", P_GW, 4), ("gn_b", P_GB, 4)):
                load(par[at:at + n, :], row(name, n), "ld_par")
            load(par[P_RK:P_RK + 4, :], A["r_k"][0].rearrange("(c a) d -> c (a d)", a=2), "ld_par")
            load(ss[:NB, :], A["state_shift"][0], "ld_ss")
            load(wlora[0:64, 0, :], A["w_decay_up"][0], "ld_lora")
            load(wlora[64:128, 0, :], A["w_a_up"][0], "ld_lora")
            load(wlora[:, 1, :], A["w_g_up"][0], "ld_lora")
            load(relb[:32, :], A["rel_bias"], "ld_bias")
            load(hot_p[:32], A["c_hot_p"], "ld_bias")
            load(log_p[:H], A["c_log_p"], "ld_bias")
            load(hot_s[:32], A["c_hot_s"], "ld_bias")
            load(log_s[:64], A["c_log_s"], "ld_bias")

            def evacuate(job, dst, src, func=ACT.Copy, **kw):
                take(act, job)
                A_.free(nc.scalar.activation(dst, src, func, **kw), job)

            def root(sums, name):
                for m in range(NM):
                    n = ROWS[m]
                    A_.ready(nc.scalar.activation(rs1[:n, m:m + 1], sums[:n, m:m + 1], ACT.Sqrt, bias=eps[:n], scale=1.0 / D), name, m + 1)

            act.wait_ge(S_("eps"), 1)
            act.wait_ge(S_("ld_x"), 48)
            for m in range(NM):
                n = ROWS[m]
                A_.ready(nc.scalar.activation(XS[:n, m, :], X[:n, m, :], ACT.Square, accum_out=sq1[:n, m:m + 1]),
                         "sumsq", m + 1)
            root(sq1, "rms1")
            evacuate("par", parT, psum("par", P_N))
            evacuate("ssT", ssT, psum("ssT", CR, NB))
            def project(*groups):
                for n in [g * GC + j for g in groups for j in range(GC)]:
                    job = f"pr{n}"
                    if n < CA:
                        evacuate(job, qkvT[:, n, :], psum(job, T))
                    elif n < CA + CR:
                        evacuate(job, rcT[:, n - CA, :], psum(job, T))
                    else:
                        evacuate(job, sgT[:, n - CA - CR, :], psum(job, T), ACT.Sigmoid)

            project(2, 3, 4, 0)
            act.wait_ge(S_("xr_ready"), 1)
            A_.ready(nc.scalar.activation(xr[0:64, 12, :], xr[0:64, 12, :], ACT.Tanh), "lora_in", 1)
            A_.ready(nc.scalar.activation(xr[:, 13, :], xr[:, 13, :], ACT.Sigmoid), "lora_in", 2)
            act.wait_ge(S_("scan_zero"), 1)
            for c in range(4):
                job = f"lw{c}"
                take(act, job)
                col = parT[:, P_W0 + c:P_W0 + c + 1]
                A_(nc.scalar.activation(sgs[:, c, :], psum(job, T)[:, S:T], ACT.Sigmoid, bias=col))
                dst = scanX[:, c * NCH:(c + 1) * NCH, CH:2 * CH]
                A_.free(nc.scalar.activation(dst, psum(job, T)[:, 0:S].rearrange("p (a b) -> p a b", b=CH),
                                             ACT.Sigmoid, bias=col), job)
            for c in range(4):
                evacuate(f"la{c}", aT[:, c, :], psum(f"la{c}", T), ACT.Sigmoid, bias=parT[:, P_A0 + c:P_A0 + c + 1])
            for c in range(4):
                evacuate(f"lg{c}", gT_[:, c, :], psum(f"lg{c}", T))
            project(1)
            act.wait_ge(S_("kk_max"), 1)
            A_.ready(nc.scalar.activation(bT, bT, ACT.Sqrt), "kk_norm", 1)
            act.wait_ge(S_("scan_done"), 1)
            cur = scanY[:, :, CH:2 * CH]
            prv = scanY[:, :, CH - 1:2 * CH - 1]
            r3 = lambda t: t.rearrange("p c (n b) -> p (c n) b", b=CH)
            A_.ready(nc.scalar.activation(r3(e[0]), cur, ACT.Exp, scale=-DECAY), "decays", 1)
            A_.ready(nc.scalar.activation(r3(e[1]), prv, ACT.Exp, scale=-DECAY), "decays", 2)
            A_.ready(nc.scalar.activation(r3(e[2]), cur, ACT.Exp, scale=DECAY), "decays", 3)
            act.wait_ge(S_("rest_sum"), 1)
            A_.ready(nc.scalar.activation(e[3], e[3], ACT.Exp, scale=-DECAY), "decays", 4)
            A_.ready(nc.scalar.activation(svT[:, 0], sgs, ACT.Exp, scale=-DECAY), "decays", 5)

            project(5, 6)
            evacuate("qn", qn[:NB, :], psum("qn", 512, parts=NB))
            act.dma_start(qn_d, qn[:NB, :]).then_inc(S_("st_qn"), 16)
            act.wait_ge(S_("st_qn"), 16)
            act.dma_start(own, A["c_own"]).then_inc(S_("ld_own"), 16)
            act.dma_start(qB, qn_d.unsqueeze(0).broadcast_to([128, NB, 512])).then_inc(S_("ld_qB"), 16)
            for m in range(NM):
                evacuate(f"kn{m}", kn[:ROWS[m], m, :], psum(f"kn{m}", 512, parts=ROWS[m]))
            for m in range(NM):
                evacuate(f"vn{m}", vn[:ROWS[m], m, :], psum(f"vn{m}", 512, parts=ROWS[m]))
            for name, t in (("k", kn), ("v", vn)):
                for m in range(2):
                    act.dma_start(O[f"p{name}"][0, 0, m * 128:(m + 1) * 128].rearrange("s h d -> s (h d)"),
                                  t[:, m, :]).then_inc(S_("st_out"), 16)
                act.dma_start(O[f"s{name}"][0, :, 0].rearrange("b h d -> b (h d)"), t[:NB, 2, :]).then_inc(S_("st_out"), 16)
            for h in range(H):
                act.wait_ge(S_("scores"), h + 1)
                for t, (c0, c1) in enumerate(((0, 128), (128, 384))):
                    v = ssb[:, h % 2, c0:c1]
                    ins = nc.scalar.activation(v, v, ACT.Exp, bias=negm[:, h, t:t + 1], accum_out=lsum[:, h, t:t + 1])
                    A_.ready(ins, "probs", 2 * h + t + 1)
                if h >= 2:
                    take(act, f"ov{h // 2 - 1}")
                evacuate(f"pt{h}", ptb[:, h % 2, :], psum(f"pt{h}", 384))
            act.wait_ge(S_("s_scores"), 1)
            A_.ready(nc.scalar.activation(s64[:64], s64[:64], ACT.Exp, bias=nms[:64], accum_out=lss[:64]), "s_probs", 1)
            act.wait_ge(S_("pts_zero"), 1)
            take(act, "spt")
            for t in range(3):
                ins = nc.scalar.activation(pts[:KT[t], t, :, 0:H], psum("spt", 3, NB, H)[:KT[t], t], ACT.Copy)
                A_.free(ins, "spt") if t == 2 else A_(ins)
            for v in range(6):
                evacuate(f"sx{v}", svn[:NB, v, :], psum(f"sx{v}", 512, parts=NB))
            act.dma_start(sv_d, svn[:NB]).then_inc(S_("st_sv"), 16)
            for m in range(2):
                evacuate(f"tV{m}", natV[:, m, :], psum(f"tV{m}", 512))
                evacuate(f"tK{m}", natK[:, m, :], psum(f"tK{m}", 512))
            for k, dst in (("A2T", aA2T), ("LX", aAT), ("LX2", aA2), ("AV", None), ("HG", None)):
                for g, (m, pr) in enumerate(GRP):
                    job = f"{k}{m}{pr}"
                    if k == "AV":
                        evacuate(job, AV[:, g], psum(job, 4, 64))
                    elif k == "HG":
                        evacuate(job, HG[:, g], psum(job, 4, 128))
                    else:
                        evacuate(job, dst[:, g], psum(job, 4, 128))
            act.wait_ge(S_("std_zero"), 2)
            for c in range(NCH):
                act.wait_ge(S_("state"), c + 1)
                if c < NCH - 1:
                    d = STd[:, c] if c < 4 else STe[:, c - 4]
                    A_(nc.scalar.activation(d[0:64, :, 0:64], stc[c][0:64], ACT.Copy))
                    A_.ready(nc.scalar.activation(d[64:128, :, 64:128], stc[c][64:128], ACT.Copy), "std", c + 1)
            evacuate("wkv", wkvn[:64], psum("wkv", 4, 128, parts=64))
            act.dma_start(O["pwkv"][0, 0].rearrange("(c a) v k -> v c a k", a=2),
                          wkvn[:64].rearrange("p c (a k) -> p c a k", a=2)).then_inc(S_("st_wkv"), 16)
            act.wait_ge(S_("gn_var"), 1)
            A_.ready(nc.scalar.activation(e4w, e4w, ACT.Sqrt), "gn_std", 1)
            for m in range(NM):
                n = ROWS[m]
                act.wait_ge(S_("x2"), m + 1)
                A_.ready(nc.scalar.activation(h2[:n, m, :], acc[:n, m, :], ACT.Square, accum_out=sq1[:n, m:m + 1]), "sumsq2", m + 1)
            root(sq1, "rms2")
            for m in range(NM):
                for g in range(2):
                    evacuate(f"ht{m}{g}", h2T[:, 4 * g:4 * g + 4, m * 128:m * 128 + ROWS[m]], psum(f"ht{m}{g}", 4, ROWS[m]))
            act.wait_ge(S_("sel_r"), 1)
            for m in range(NM):
                n = ROWS[m]
                A_.ready(nc.scalar.activation(rexp[:n, m, :], lgt[:n, m, 0:NE], ACT.Exp, bias=ngm[:n, m:m + 1]), "r_exp", m + 1)
            evacuate("gT", gateT[:NE], psum("gT", NM, 128, parts=NE))
            act.wait_ge(S_("st_wkv"), 16)
            act.wait_ge(S_("moe_zero"), 1)
            act.wait_ge(S_("npass"), 1)
            nc.scalar.activation(lss[:1], lss[:1], ACT.Copy).then_inc(S_("y_out"), 1)
            act.wait_ge(S_("y_out"), 1)
            nc.scalar.activation(lss[:1], lss[:1], ACT.Copy).then_inc(S_("selgT_out"), 1)
            passes = act.value_load(npass[0:1, 0:1], min_val=1, max_val=PASSES)

            def gathered(it):
                act.wait_ge(S_("xg_full"), it + 1)
                nc.scalar.activation(xg, PS[0][:, :], ACT.Copy).then_inc(S_("xg_out"), 1)

            def gathered_T(it):
                act.wait_ge(S_("xgT_full"), it + 1)
                nc.scalar.activation(xgT, PS[1][:, :].rearrange("p (c s) -> p c s", c=4), ACT.Copy).then_inc(S_("xgT_out"), 1)

            gathered(0)
            gathered_T(0)
            with act.Fori(0, passes) as p:
                with act.Fori(0, NE) as ex:
                    it = act.snap(p * NE + ex)
                    act.wait_ge(S_("gt"), it + 1)
                    nc.scalar.activation(sg, gt, ACT.Sigmoid, scale=ALPHA).then_inc(S_("sg"), 1)
                    gathered(it + 1)
                    act.wait_ge(S_("selgT_full"), it + 1)
                    nc.scalar.activation(selgT, PS[5][:, 0:384], ACT.Copy).then_inc(S_("selgT_out"), 1)
                    gathered_T(it + 1)
                    act.wait_ge(S_("actT_full"), it + 1)
                    nc.scalar.activation(actT, PS[4][:, :].rearrange("p (c s) -> p c s", c=4), ACT.Copy).then_inc(S_("actT_out"), 1)
                    act.wait_ge(S_("unit_used"), it * 12 + 24)
                    nc.scalar.activation(yS, PS[5][:, :], ACT.Copy).then_inc(S_("y_out"), 1)
            act.wait_ge(S_("acc_final"), 1)
            for m in range(NM):
                n = ROWS[m]
                A_.ready(nc.scalar.activation(h2[:n, m, :], acc[:n, m, :], ACT.Square, accum_out=sq1[:n, m:m + 1]), "sumsq3", m + 1)
            root(sq1, "rms3")
            for m in range(2):
                act.wait_ge(S_("y"), m + 1)
                act.dma_start(O["yp"][0, m * 128:(m + 1) * 128, :], acc[:, m, :]).then_inc(S_("st_y"), 16)
            act.wait_ge(S_("y"), 3)
            act.dma_start(O["ys"][:, 0, :], acc[:NB, 2, :]).then_inc(S_("st_y"), 16)
            act.wait_ge(S_("st_y"), 48)

        @block.gpsimd
        def _(pool):
            G_ = Chain(pool, "pool_step")
            pool.wait_ge(S_("ld_bias"), 16 * 5)
            G_.ready(nc.gpsimd.tensor_copy(relb64[:32], bc(relb[:32], 1, NB)), "relb64", 1)
            pool.wait_ge(S_("bvec"), 1)
            pool.dma_start(bvec_d, bc(bvec[:H], 1, 128)).then_inc(S_("st_bv"), 16)
            pool.wait_ge(S_("st_bv"), 16)
            pool.dma_start(B3[:, :, 128:384], bass.AP(bvec_d.tensor, 127, [[NREL - 1, 128], [128 * NREL, H], [1, 256]])).then_inc(S_("ld_B3"), 16)
            pool.dma_start(B3[:, :, 0:128], bass.AP(bvec_d.tensor, 255, [[NREL - 1, 128], [128 * NREL, H], [1, 128]])).then_inc(S_("ld_B3"), 16)
            pool.wait_ge(S_("shn"), 1)
            pool.dma_start(O["pshift"][0], shn[0:1, :]).then_inc(S_("st_sh"), 16)
            pool.dma_start(O["sshift"][0], shn[1:9, :]).then_inc(S_("st_sh"), 16)
            pool.wait_ge(S_("ld_qB"), 16)
            for i in range(NB):
                b = i
                pool.wait_ge(S_(f"ld_k{b % 2}"), 64 * (b // 2 + 1))
                if b >= 2:
                    pool.wait_ge(S_("s_red"), b - 1)
                G_.ready(nc.gpsimd.tensor_tensor(PROD[b % 2], Kb[b % 2],
                                                 bc(qB[:, b, :], 1, 3), ALU.mult), "pool_prod", b + 1)
            pool.wait_ge(S_("st_sv"), 16)
            srcv = sv_d.rearrange("b x (h d) -> b h x d", h=H)
            for vh in range(2):
                for b in range(NB):
                    p0 = vh * 64 + b * H
                    pool.dma_start(svec[p0:p0 + H], srcv[b]).then_inc(S_("ld_svec"), 16)
            sw = A["state_wkv"][0].rearrange("b h v k -> (b h) v k")
            ow = O["swkv"][0].rearrange("b h v k -> (b h) v k")
            pool.wait_ge(S_("ld_svec"), 16 * 16)
            over_v = lambda t: bc(t, 1, 16)
            over_k = lambda t: bc(t, 2, E64)
            vw, vk, vb_, vkr, vv, vr_ = range(6)
            for q in range(2):
                for vh in range(2):
                    v0 = vh * 32 + q * 16
                    pool.dma_start(S1[vh * 64:vh * 64 + 64], sw[:, v0:v0 + 16, :]).then_inc(S_("ld_S"), 16)
                pool.wait_ge(S_("ld_S"), 32 * (q + 1))
                tt = nc.gpsimd.tensor_tensor
                G_(tt(S1t, S1, over_v(svec[:, vk]), ALU.mult))
                G_.ready(nc.gpsimd.tensor_tensor(S1, S1, over_v(svec[:, vw]), ALU.mult), "s_t1", q + 1)
                pool.wait_ge(S_("s_u1"), q + 1)
                G_(tt(S1t, over_k(u1), over_v(svec[:, vb_]), ALU.mult))
                G_(tt(S1, S1, S1t, ALU.subtract))
                for vh in range(2):
                    ps_ = slice(vh * 64, vh * 64 + 64)
                    v0 = vh * 32 + q * 16
                    G_(tt(S1t[ps_], over_k(svec[ps_, vv, v0:v0 + 16]), over_v(svec[ps_, vkr]), ALU.mult))
                G_(tt(S1, S1, S1t, ALU.add))
                for vh in range(2):
                    v0 = vh * 32 + q * 16
                    pool.dma_start(ow[:, v0:v0 + 16, :], S1[vh * 64:vh * 64 + 64]).then_inc(S_("st_S"), 16)
                G_.ready(tt(S1t, S1, over_v(svec[:, vr_]), ALU.mult), "s_t2", q + 1)
                pool.wait_ge(S_("s_y"), q + 1)
                pool.wait_ge(S_("st_S"), 32 * (q + 1))
            pool.dma_start(ys_d.rearrange("a r v -> (a r) v"), ysm.rearrange("p a b -> p (a b)")).then_inc(S_("st_ys"), 16)
            pool.wait_ge(S_("st_ys"), 16)
            pool.dma_start(ysn[:NB].rearrange("b (h a v) -> b h a v", h=H, a=2),
                           ys_d.rearrange("a (b h) v -> b h a v", b=NB)).then_inc(S_("ld_ysn"), 16)
            pool.wait_ge(S_("st_sh"), 32)

        @block.vector
        def _(dve):
            V = Chain(dve, "dve_step")
            v = nc.vector

            def tt(out, a, b, op):
                return v.tensor_tensor(out, a, b, op)

            def parc(at, n=4, width=T):
                return bc(parT[:, at:at + n], 2, width)

            V.ready(v.memset(eps, 1e-6), "eps", 1)
            dve.wait_ge(S_("ld_x"), 48)
            for m in range(NM):
                n = ROWS[m]
                dve.wait_ge(S_("rms1"), m + 1)
                V(v.reciprocal(rs1[:n, m:m + 1], rs1[:n, m:m + 1]))
                V.ready(v.tensor_scalar(XS[:n, m, :], X[:n, m, :], rs1[:n, m:m + 1], None, ALU.mult), "xs", m + 1)
            after(dve, "par")
            for m in range(NM):
                n = ROWS[m]
                for g in range(2):
                    job = f"hT{m}{g}"
                    take(dve, job)
                    V.free(tt(hT[:, g * 4:(g + 1) * 4, m * 128:m * 128 + n], psum(job, 4, n),
                              parc(P_LN1 + 4 * g, 4, n), ALU.mult), job)
            V(v.memset(RING[96:128, 18432:24576], 0.0))
            V.ready(v.memset(mcount, 0.0), "kv_zero", 1)
            after(dve, "ssT", *[f"pr{CA + c}" for c in range(CR)])
            V(tt(xr[:, :, 1:S], rcT[:, :, 0:S - 1], rcT[:, :, 1:S], ALU.subtract))
            V(v.tensor_scalar(xr[:, :, 0:1], rcT[:, :, 0:1], -1.0, None, ALU.mult))
            V(tt(xr[:, :, S:T], ssT, rcT[:, :, S:T], ALU.subtract))
            V(tt(xr, xr, parc(P_MU, CR), ALU.mult))
            V.ready(tt(xr, xr, rcT, ALU.add), "xr_ready", 1)
            take(dve, "bvp")
            V.free(tt(bvec[:H], psum("bvp", NREL, parts=H), log_p[:H], ALU.add), "bvp")
            take(dve, "bvs")
            V.free(tt(biasS[:64], psum("bvs", NKEY, parts=64), log_s[:64], ALU.add), "bvs")
            V.ready(v.memset(mcount, 0.0), "bvec", 1)
            for g in range(4):
                job, n = f"sh{g}", (4 if g < 3 else 2) * 128
                take(dve, job)
                V.free(v.tensor_copy(shn[:9, g * 512:g * 512 + n], psum(job, n, parts=9)), job)
            V.ready(v.memset(scanX[:, :, 0:CH], 0.0), "shn", 1)
            dve.wait_ge(S_("st_sh"), 32)
            V(v.memset(scanY[:, :, 0:CH], 0.0))
            V.ready(v.memset(mcount, 0.0), "scan_zero", 1)
            after(dve, *[f"lw{c}" for c in range(4)])
            src, dst = scanX, scanY
            for i, reach in enumerate((1, 2, 4, 8, 16)):
                ins = tt(dst[:, :, CH:2 * CH], src[:, :, CH:2 * CH], src[:, :, CH - reach:2 * CH - reach], ALU.add)
                V.ready(ins, "scan_done", 1) if i == 4 else V(ins)
                src, dst = dst, src
            r3 = lambda t: t.rearrange("p c (n b) -> p (c n) b", b=CH)
            V.ready(tt(r3(e[3]), scanY[:, :, 2 * CH - 1:2 * CH].broadcast_to([128, 4 * NCH, CH]),
                       scanY[:, :, CH:2 * CH], ALU.subtract), "rest_sum", 1)
            rT, kT, vT = xr[:, 0:4], xr[:, 4:8], xr[:, 8:12]
            V(tt(kkn, kT, parc(P_KK), ALU.mult))
            V.ready(tt(bT, kkn, kkn, ALU.mult), "kk_sq", 1)
            after(dve, *[f"la{c}" for c in range(4)])
            for c in range(4):
                take(dve, f"nk{c}")
                V.free(v.tensor_scalar(bT[:, c, :], psum(f"nk{c}", T), 1e-24, None, ALU.max), f"nk{c}")
            V.ready(v.memset(mcount, 0.0), "kk_max", 1)
            V(v.scalar_tensor_tensor(e4w, aT, -1.0, kT, ALU.add, ALU.mult))
            V(tt(e4w, e4w, parc(P_KA), ALU.mult))
            V(tt(kT, kT, e4w, ALU.add))
            dve.wait_ge(S_("kk_norm"), 1)
            V(v.reciprocal(bT, bT))
            V(tt(kkn, kkn, bT, ALU.mult))
            V(tt(bT, kkn, aT, ALU.mult))
            dve.wait_ge(S_("decays"), 5)
            for i, t in enumerate((kkn, bT, kT, vT, rT)):
                V(v.tensor_copy(svT[:, 1 + i], t[:, :, S:T]))
            V(v.tensor_copy(pcs, e[0][:, :, CH - 1:S:CH]))
            V(tt(e[1], kkn[:, :, 0:S], e[1], ALU.mult))
            V(tt(e[0], rT[:, :, 0:S], e[0], ALU.mult))
            V(tt(e[5], kT[:, :, 0:S], e[2], ALU.mult))
            V(tt(e[2], bT[:, :, 0:S], e[2], ALU.mult))
            V(tt(e[4], kT[:, :, 0:S], e[3], ALU.mult))
            V.ready(v.scalar_tensor_tensor(e[3], e[3], -1.0, bT[:, :, 0:S], ALU.mult, ALU.mult), "products", 1)
            V(tt(bT, rT, kT, ALU.mult))
            V.ready(tt(bT, bT, parc(P_RK), ALU.mult), "rk", 1)

            def score(h):
                take(dve, f"s{h}")
                if h >= 2:
                    take(dve, f"pt{h - 2}")
                w = ssb[:, h % 2, :]
                V.free(v.scalar_tensor_tensor(w, psum(f"s{h}", 384), SCALE, B3[:, h, :], ALU.mult, ALU.add), f"s{h}")
                V(v.tensor_reduce(negm[:, h, 0:1], w[:, 0:128], AX.X, ALU.max, negate=True))
                V.ready(v.tensor_reduce(negm[:, h, 1:2], w[:, 128:384], AX.X, ALU.max, negate=True), "scores", h + 1)

            def normalise(h):
                dve.wait_ge(S_("probs"), 2 * h + 2)
                V(v.reciprocal(rinv[:, h, :], lsum[:, h, :]))
                V(v.tensor_scalar(ssb[:, h % 2, 0:128], ssb[:, h % 2, 0:128], rinv[:, h, 0:1], None, ALU.mult))
                V.ready(v.tensor_scalar(ssb[:, h % 2, 128:384], ssb[:, h % 2, 128:384], rinv[:, h, 1:2], None, ALU.mult),
                        "pn", h + 1)

            def reduce_b(b):
                dve.wait_ge(S_("pool_prod"), b + 1)
                src = PROD[b % 2].rearrange("p t (h d) -> p t h d", h=H)
                V.ready(v.tensor_reduce(scs[:, :, b * H:(b + 1) * H], src, AX.X, ALU.add),
                        "s_red", b + 1)

            V.ready(v.memset(pts, 0.0), "pts_zero", 1)
            dve.wait_ge(S_("ld_B3"), 32)
            score(0)
            for h in range(H):
                if h + 1 < H:
                    score(h + 1)
                normalise(h)
                if h >= 3 and h % 2:
                    take(dve, f"ov{h // 2 - 1}")
                    V.free(v.tensor_copy(oaT[:, h // 2 - 1, 0:S], psum(f"ov{h // 2 - 1}", S)), f"ov{h // 2 - 1}")
                reduce_b(h)
            take(dve, "ov3")
            V.free(v.tensor_copy(oaT[:, 3, 0:S], psum("ov3", S)), "ov3")
            take(dve, "sst")
            V.free(v.scalar_tensor_tensor(s64[:64], psum("sst", NKEY, parts=64), SCALE, biasS[:64], ALU.mult, ALU.add), "sst")
            V.ready(v.tensor_reduce(nms[:64], s64[:64], AX.X, ALU.max, negate=True), "s_scores", 1)
            dve.wait_ge(S_("s_probs"), 1)
            V(v.reciprocal(ris[:64], lss[:64]))
            V.ready(v.tensor_scalar(s64[:64], s64[:64], ris[:64], None, ALU.mult), "s_pn", 1)
            dve.wait_ge(S_("ld_own"), 16)
            for g in range(2):
                take(dve, f"pv{g}")
                V.free(tt(pvm[:, g, :], psum(f"pv{g}", 512), own, ALU.mult), f"pv{g}")
            take(dve, "sv")
            V.free(v.tensor_copy(oaT[:, :, S:T], psum("sv", 4, NB)), "sv")
            for c in range(4):
                take(dve, f"bo{c}")
                V.free(tt(bT[:, c, :], psum(f"bo{c}", T), vT[:, c, :], ALU.mult), f"bo{c}")
            for m in range(2):
                for k, dst in (("tC", natC), ("tB", natB)):
                    take(dve, f"{k}{m}")
                    V.free(v.tensor_copy(dst[:, m, :], psum(f"{k}{m}", 512)), f"{k}{m}")

            dve.wait_ge(S_("st_out"), 16 * 6)
            dve.wait_ge(S_("st_sh"), 32)
            def masked(kind, *pairs):
                for g, (m, pr) in enumerate(GRP):
                    job = f"{kind}{m}{pr}"
                    take(dve, job)
                    for n, (dst, mask) in enumerate(pairs):
                        ins = tt(dst[:, g], psum(job, 4, 128), bc(C[mask], 1, 4), ALU.mult)
                        V.free(ins, job) if n == len(pairs) - 1 else V(ins)

            masked("Auk", (aAuk, "strict"))
            masked("Brk", (aBrk, "incl"))
            masked("Aub", (aAT, "up8"), (aL1T, "up16"), (aL2T, "up32"))
            masked("Brb", (aBrb, "neg_incl"))
            masked("A8", (aA, "lo8"))

            def each(kind, fn):
                for g, (m, pr) in enumerate(GRP):
                    job = f"{kind}{m}{pr}"
                    take(dve, job)
                    V.free(fn(g, psum(job, 4, 128)), job)

            def sample_sum(kind, q):
                dve.wait_ge(S_("s_t1" if kind == "u" else "s_t2"), q + 1)
                if kind == "u":
                    V.ready(v.tensor_reduce(u1, S1t, AX.X, ALU.add), "s_u1", q + 1)
                else:
                    V.ready(v.tensor_reduce(ysm[:, q, :], S1t, AX.X, ALU.add), "s_y", q + 1)

            for g, (m, pr) in enumerate(GRP):
                job = f"A2{m}{pr}"
                take(dve, job)
                V(v.tensor_copy(aA2[:, g], psum(job, 4, 128)))
                V.free(tt(aI[:, g], psum(job, 4, 128), bc(C["ident"], 1, 4), ALU.add), job)
            for g, (m, pr) in enumerate(GRP):
                take(dve, f"A2T{m}{pr}")
                V.ready(tt(aAT[:, g], bc(C["ident"], 1, 4), aAT[:, g], ALU.subtract), "imat", g + 1)
            each("X1T", lambda g, p: v.tensor_copy(aA[:, g], p))
            each("A4", lambda g, p: tt(aI[:, g], p, bc(C["ident"], 1, 4), ALU.add))
            each("X", lambda g, p: v.tensor_copy(aA2[:, g], p))
            each("XT", lambda g, p: v.tensor_copy(aA2T[:, g], p))
            sample_sum("u", 0)
            each("X2", lambda g, p: tt(aA[:, g], aA2[:, g], p, ALU.subtract))
            each("X2T", lambda g, p: tt(aI[:, g], aA2T[:, g], p, ALU.subtract))
            sample_sum("y", 0)
            take(dve, "LX211")
            V(v.memset(TT[0:64, :, :, 64:128], 0.0))
            V(v.memset(TT[64:128, :, :, 0:64], 0.0))
            V.ready(v.memset(STd, 0.0), "std_zero", 1)
            each("MT", lambda g, p: tt(aA2T[:, g], aI[:, g], p, ALU.subtract))
            V.ready(v.memset(STe, 0.0), "std_zero", 2)
            sample_sum("u", 1)
            for kind in ("Y0", "Rp"):
                for g, (m, pr) in enumerate(GRP):
                    job = f"{kind}{m}{pr}"
                    take(dve, job)
                    q = slice(pr * 64, pr * 64 + 64)
                    tok = slice(m * 128, m * 128 + 128)
                    if kind == "Y0":
                        V.free(v.tensor_copy(Y0[q, :, tok], psum(job, 4, 128)[q]), job)
                    else:
                        V.free(tt(Rp[q, :, tok], psum(job, 4, 128)[q], e[0][q, :, tok], ALU.add), job)
            for c in range(NCH):
                job = f"TZ{c}"
                if c:
                    V(tt(dtmp, bc(C["idstack"][:, 0:64], 1, 4), pcs[:, :, c:c + 1].broadcast_to([128, 4, 64]), ALU.mult))
                take(dve, job)
                p2 = psum(job, 2, 4, 64)
                if c:
                    V(tt(TT[0:64, c, :, 0:64], p2[0:64, 0], dtmp[0:64], ALU.add))
                    V(tt(TT[64:128, c, :, 64:128], p2[64:128, 0], dtmp[64:128], ALU.add))
                V.free(v.tensor_copy(Zc[:, c], p2[:, 1]), job)
            V.ready(v.tensor_copy(stc[0], Zc[:, 0]), "state", 1)
            for c in range(1, NCH):
                job = f"st{c}"
                take(dve, job)
                V.free(tt(stc[c], psum(job, 4, 64), Zc[:, c], ALU.add), job)
                V.ready(v.memset(mcount, 0.0), "state", c + 1)
            sample_sum("y", 1)
            V(v.tensor_copy(YT[:, :, 0:CH], Y0[:, :, 0:CH]))
            for c in range(1, NCH):
                job = f"yt{c}"
                take(dve, job)
                V.free(tt(YT[:, :, c * CH:(c + 1) * CH], psum(job, 4, CH), Y0[:, :, c * CH:(c + 1) * CH], ALU.add), job)
            take(dve, "sy")
            V.free(v.tensor_copy(YT[:, :, S:T], psum("sy", 4, NB)), "sy")
            for c in range(4):
                take(dve, f"mu{c}")
                V.free(tt(YT[:, c, :], YT[:, c, :], psum(f"mu{c}", T), ALU.subtract), f"mu{c}")
            V.ready(tt(e4w, YT, YT, ALU.mult), "y_sq", 1)
            for c in range(4):
                take(dve, f"va{c}")
                V.free(v.tensor_scalar(e4w[:, c, :], psum(f"va{c}", T), 64e-5, None, ALU.add), f"va{c}")
            V.ready(v.memset(mcount, 0.0), "gn_var", 1)
            dve.wait_ge(S_("gn_std"), 1)
            V(v.reciprocal(e4w, e4w))
            V(tt(YT, YT, e4w, ALU.mult))
            V(tt(YT, YT, parc(P_GW), ALU.mult))
            V(tt(YT, YT, parc(P_GB), ALU.add))
            V(tt(YT, YT, bT, ALU.add))
            V.ready(tt(YT, YT, gT_, ALU.mult), "obT", 1)
            for d in range(KD):
                for n, k in enumerate(("ma", "mb")):
                    job = f"{k}{d}"
                    take(dve, job)
                    w = sgT[:, n * KD + d, :]
                    V.free(tt(w, psum(job, T), w, ALU.mult), job)
                V.ready(tt(mixT[:, d, :], sgT[:, d, :], sgT[:, KD + d, :], ALU.add), "mix", d + 1)
            V.ready(v.memset(brow, 0.0), "brow_zero", 1)
            dve.wait_ge(S_("ld_acc"), 48)
            V(v.memset(h2[:, 2, :], 0.0))
            for m in range(NM):
                n = ROWS[m]
                for g in range(2):
                    job = f"wo{m}{g}"
                    take(dve, job)
                    a = acc[:n, m, g * 512:(g + 1) * 512]
                    V.free(tt(a, psum(job, 512, parts=n), a, ALU.add), job)
                V.ready(v.memset(mcount, 0.0), "x2", m + 1)
            dve.wait_ge(S_("ld_ln"), 32)
            for m in range(NM):
                n = ROWS[m]
                dve.wait_ge(S_("rms2"), m + 1)
                V(v.reciprocal(rs1[:n, m:m + 1], rs1[:n, m:m + 1]))
                V.ready(v.scalar_tensor_tensor(h2[:n, m, :], acc[:n, m, :], rs1[:n, m:m + 1], ln2b[:n], ALU.mult, ALU.mult),
                        "h2", m + 1)
            V(v.memset(lgt, BIG))
            V(v.memset(selr, 0.0))
            V(v.memset(gate, 0.0))
            take(dve, "lg")
            for m in range(NM):
                n = ROWS[m]
                V(tt(lgt[:n, m, 0:NE], psum("lg", NM, NE)[:n, m, :], brow_r[:n], ALU.add))
                V(v.max(max8[:n, m, :], lgt[:n, m, :]))
                V(v.match_replace(rep[:n, m, :], max8[:n, m, :], lgt[:n, m, :], NEG))
                V(v.tensor_scalar(selr[:n, m, :], rep[:n, m, 0:NE], NEG, None, ALU.is_equal))
                ins = v.tensor_scalar(ngm[:n, m:m + 1], max8[:n, m, 4:5], -1.0, None, ALU.mult)
                V.free(ins, "lg") if m == 2 else V(ins)
            V.ready(v.memset(mcount, 0.0), "sel_r", 1)
            dve.wait_ge(S_("r_exp"), 3)
            for m in range(NM):
                n = ROWS[m]
                V(tt(gate[:n, m, :], rexp[:n, m, :], selr[:n, m, :], ALU.mult))
                V(v.tensor_reduce(gsum[:n, m:m + 1], gate[:n, m, :], AX.X, ALU.add))
                V(v.reciprocal(gsum[:n, m:m + 1], gsum[:n, m:m + 1]))
                V.ready(v.tensor_scalar(gate[:n, m, :], gate[:n, m, :], gsum[:n, m:m + 1], None, ALU.mult), "gate", m + 1)
            take(dve, "rk")
            V(v.memset(posx, 0.0))
            for m in range(NM):
                V(v.scalar_tensor_tensor(posx[:, m, 0:NE], psum("rk", 4, NE)[:, m, :], 1.0, selr[:, m, :], ALU.add, ALU.mult))
            for b in range(1, PASSES):
                V(v.tensor_scalar(posx[:, :, b * NE:(b + 1) * NE], posx[:, :, 0:NE], float(-SLOT * b), None, ALU.add))
            V.free(v.tensor_reduce(mcount, psum("rk", 4, NE)[:, 3, :], AX.X, ALU.max), "rk")
            V(v.memset(thr, 1.0))
            for b in range(1, PASSES):
                V(v.tensor_scalar(thr[:, b:b + 1], mcount, float(SLOT * b), None, ALU.is_gt))
            V(v.tensor_reduce(mcount, thr, AX.X, ALU.add))
            V.ready(v.tensor_copy(npass[:, :], mcount), "npass", 1)
            for m in range(NM):
                n = ROWS[m]
                for g in range(2):
                    job = f"bd{m}{g}"
                    take(dve, job)
                    a = acc[:n, m, g * 512:(g + 1) * 512]
                    V.free(tt(a, psum(job, 512, parts=n), a, ALU.add), job)
            V(v.memset(sel, 0.0))
            V(v.memset(selg, 0.0))
            V(v.memset(yS, 0.0))
            V.ready(v.memset(selgT, 0.0), "moe_zero", 1)
            for m in range(NM):
                ins = v.tensor_scalar(sel[:ROWS[m], m, :], C["slots"][:ROWS[m], 0:SLOT], posx[:ROWS[m], m, 0:1], None, ALU.is_equal)
                V.ready(ins, "sel", 1) if m == 2 else V(ins)
            passes = dve.value_load(npass[0:1, 0:1], min_val=1, max_val=PASSES)
            V(v.memset(mcount, 0.0))
            dve.sem_inc(S_("acc_done"), 2)
            dve.wait_ge(S_("acc_done"), 2)

            def accumulate(it, m):
                n = ROWS[m]
                dve.wait_ge(S_("cmb_full"), it * 3 + (m + 1))
                for g in range(2):
                    a = acc[:n, m, g * 512:(g + 1) * 512]
                    tt(a, PS[CMB[m][g]][:n, :], a, ALU.add).then_inc(S_("acc_done"), 1)

            with dve.Fori(0, passes) as p:
                with dve.Fori(0, NE) as ex:
                    it = dve.snap(p * NE + ex)
                    dve.wait_ge(S_("gu_full"), it + 1)
                    v.tensor_scalar(gt, PS[2][:, :], LIMIT, None, ALU.min).then_inc(S_("gt"), 1)
                    v.tensor_scalar(up, PS[3][:, :], LIMIT, -LIMIT, ALU.min, ALU.max).then_inc(S_("up"), 1)
                    for m in range(NM):
                        n = ROWS[m]
                        v.tensor_scalar(sel[:n, m, :], C["slots"][:n, 0:SLOT], posx[:n, m, bass.ds(it + 1, 1)], None,
                                        ALU.is_equal).then_inc(S_("sel_next"), 1)
                    dve.wait_ge(S_("gt"), it + 1)
                    dve.wait_ge(S_("up"), it + 1)
                    v.scalar_tensor_tensor(up, up, 1.0, gt, ALU.add, ALU.mult).then_inc(S_("upgt"), 1)
                    dve.wait_ge(S_("upgt"), it + 1)
                    dve.wait_ge(S_("sg"), it + 1)
                    tt(up, up, sg, ALU.mult).then_inc(S_("act"), 1)
                    dve.wait_ge(S_("acc_done"), it * 6 + 2)
                    accumulate(it, 0)
                    for m in range(NM):
                        n = ROWS[m]
                        v.tensor_scalar(selg[:n, m, :], C["slots"][:n], posx[:n, m, bass.ds(it, 1)],
                                        gate[:n, m, bass.ds(ex, 1)], ALU.is_equal, ALU.mult).then_inc(S_("selg"), 1)
                    accumulate(it, 1)
                    accumulate(it, 2)
            last = dve.snap(passes * NE)
            dve.wait_ge(S_("acc_done"), last * 6 + 2)
            for m in range(NM):
                accumulate(last, m)
            dve.wait_ge(S_("acc_done"), last * 6 + 8)
            v.memset(mcount, 0.0).then_inc(S_("acc_final"), 1)
            for m in range(NM):
                n = ROWS[m]
                dve.wait_ge(S_("rms3"), m + 1)
                V(v.reciprocal(rs1[:n, m:m + 1], rs1[:n, m:m + 1]))
                v.scalar_tensor_tensor(acc[:n, m, :], acc[:n, m, :], rs1[:n, m:m + 1], lnfb[:n], ALU.mult, ALU.mult)\
                 .then_inc(S_("y"), 1)

        @block.tensor
        def _(pe):
            mm = nc.tensor.matmul

            def give(job):
                if turn[job] > 1:
                    pe.wait_ge(evac[bank[job]], turn[job] - 1)

            def done(ins, job):
                ins.then_inc(full[bank[job]], 1)

            def transposes(job, pieces, width, parts=128):
                give(job)
                for n, src in enumerate(pieces):
                    rows = src.shape[0]
                    last = nc.tensor.transpose(PS[bank[job]][:parts, n * width:n * width + rows], src, C["ident"][:rows, :rows])
                done(last, job)

            pe.wait_ge(S_("ld_mats"), 16)
            pe.wait_ge(S_("ld_par"), 16 * 9)
            transposes("par", [par[:P_N, :]], P_N)
            pe.wait_ge(S_("ld_ss"), 16)
            transposes("ssT", [ss[:NB, c * 128:(c + 1) * 128] for c in range(CR)], NB)
            for m in range(NM):
                pe.wait_ge(S_("xs"), m + 1)
                for g in range(2):
                    transposes(f"hT{m}{g}", [XS[:ROWS[m], m, (4 * g + c) * 128:(4 * g + c + 1) * 128] for c in range(4)], ROWS[m])
            after(pe, "hT20", "hT21")
            def project(*groups):
                for g in groups:
                    gi = GROUPS.index(g)
                    pe.wait_ge(S_(f"ld_win{gi}"), 16)
                    for j in range(GC):
                        job = f"pr{g * GC + j}"
                        give(job)
                        for k in range(KD):
                            last = mm(psum(job, T), WIN[gi % 2][:, k, j * 128:(j + 1) * 128], hT[:, k, :], start=k == 0, stop=k == KD - 1)
                        done(last, job)

            project(2, 3, 4)
            pe.wait_ge(S_("relb64"), 1)
            give("bvp")
            done(mm(psum("bvp", NREL, parts=H), relb[:32, :], hot_p[:32], start=True, stop=True), "bvp")
            give("bvs")
            done(mm(psum("bvs", NKEY, parts=64), relb64[:32].rearrange("p a b -> p (a b)"), hot_s[:32], start=True, stop=True), "bvs")
            for g in range(4):
                transposes(f"sh{g}", [rcT[:, c, S - 1:T] for c in range(4 * g, min(4 * g + 4, CR))], 128, NB + 1)
            project(0)
            pe.wait_ge(S_("ld_lora"), 48)
            pe.wait_ge(S_("lora_in"), 2)
            for k, lo, hi, w, src in (("lw", 0, 64, 0, 12), ("la", 64, 128, 0, 12), ("lg", 0, 128, 1, 13)):
                for c in range(4):
                    give(f"{k}{c}")
                    done(mm(psum(f"{k}{c}", T), wlora[lo:hi, w, c * 128:(c + 1) * 128], xr[lo:hi, src, :], start=True, stop=True), f"{k}{c}")
            project(1)
            pe.wait_ge(S_("kk_sq"), 1)
            for c in range(4):
                give(f"nk{c}")
                done(mm(psum(f"nk{c}", T), C["head_sum"], bT[:, c, :], start=True, stop=True), f"nk{c}")
            project(5, 6)
            transposes("qn", [qkvT[:, c, S:T] for c in range(4)], 128, NB)
            for at, name in ((4, "kn"), (8, "vn")):
                for m in range(NM):
                    transposes(f"{name}{m}", [qkvT[:, at + c, m * 128:m * 128 + ROWS[m]] for c in range(4)], 128, ROWS[m])
            def score(h):
                q = slice((h % 2) * 64, (h % 2) * 64 + 64)
                give(f"s{h}")
                w = psum(f"s{h}", 384)
                mm(w[:, 0:128], qkvT[q, h // 2, 0:128], qkvT[q, 4 + h // 2, 0:128], start=True, stop=True)
                done(mm(w[:, 128:384], qkvT[q, h // 2, 128:256], qkvT[q, 4 + h // 2, 0:256], start=True, stop=True), f"s{h}")
            score(0)
            score(1)
            for h in range(H):
                if h + 2 < H:
                    score(h + 2)
                pe.wait_ge(S_("pn"), h + 1)
                transposes(f"pt{h}", [ssb[:, h % 2, 128 * t:128 * t + 128] for t in range(3)], 128)
                if h % 2:
                    job = f"ov{h // 2}"
                    give(job)
                    for hh in (h - 1, h):
                        after(pe, f"pt{hh}")
                        q = slice((hh % 2) * 64, (hh % 2) * 64 + 64)
                        mm(psum(job, S)[q, :], vn[:, 0, hh * 64:hh * 64 + 64], ptb[:, hh % 2, 0:256], start=True, stop=False)
                        last = mm(psum(job, S)[q, 128:256], vn[:, 1, hh * 64:hh * 64 + 64], ptb[:, hh % 2, 256:384], start=False, stop=True)
                    done(last, job)
            pe.wait_ge(S_("s_red"), NB)
            give("sst")
            for t in range(3):
                last = nc.tensor.transpose(PS[bank["sst"]][:64, KO[t]:KO[t] + KT[t]], scs[:KT[t], t, :], C["ident"][:KT[t], :KT[t]])
            done(last, "sst")
            pe.wait_ge(S_("s_pn"), 1)
            give("spt")
            for t in range(3):
                last = nc.tensor.transpose(PS[bank["spt"]][:KT[t], t * 64:t * 64 + 64], s64[:64, KO[t]:KO[t] + KT[t]], C["ident"][:64, :64])
            done(last, "spt")
            after(pe, "spt")
            for g in range(2):
                for j in range(4):
                    pe.wait_ge(S_(f"ld_v{j}"), 64 * (g + 1))
                job = f"pv{g}"
                give(job)
                for t in range(3):
                    for j in range(4):
                        last = mm(psum(job, 512)[32 * j:32 * j + 32], pts[:KT[t], t, 4 * g + j, :], Vb[j][:KT[t], t, :],
                                  start=t == 0, stop=t == 2)
                done(last, job)
            after(pe, "pv0", "pv1")
            give("sv")
            for c in range(4):
                for g in range(2):
                    last = mm(psum("sv", 4, 2, 4)[:, c, g, :], pvm[:, g, c * 128:(c + 1) * 128], C["quad"][:, 0:4], start=True, stop=True)
            done(last, "sv")
            pe.wait_ge(S_("rk"), 1)
            for x in range(6):
                transposes(f"sx{x}", [svT[:, x, c, :] for c in range(4)], 128, NB)
            for c in range(4):
                give(f"bo{c}")
                done(mm(psum(f"bo{c}", T), C["head_sum"], bT[:, c, :], start=True, stop=True), f"bo{c}")
            for m in range(2):
                tok = slice(m * 128, m * 128 + 128)
                transposes(f"tV{m}", [xr[:, 8 + c, tok] for c in range(4)], 128)
                transposes(f"tK{m}", [e[1][:, c, tok] for c in range(4)], 128)
                transposes(f"tC{m}", [e[4][:, c, tok] for c in range(4)], 128)
                transposes(f"tB{m}", [e[3][:, c, tok] for c in range(4)], 128)

            def heads(kind, fn, *waits):
                for g, (m, pr) in enumerate(GRP):
                    job = f"{kind}{m}{pr}"
                    for w in waits:
                        after(pe, f"{w}{m}{pr}")
                    if kind == "X1T":
                        pe.wait_ge(S_("imat"), g + 1)
                    give(job)
                    for hh in range(4):
                        last = fn(psum(job, 4, 128)[:, hh, :], g, m, pr, hh)
                    done(last, job)

            def pairs(lhs, rhs):
                def fn(out, g, m, pr, hh):
                    q = slice(pr * 64, pr * 64 + 64)
                    tok = slice(m * 128, m * 128 + 128)
                    return mm(out, lhs[q, hh, tok], rhs[q, hh, tok], start=True, stop=True)
                return fn

            def prod(lhs, rhs):
                return lambda out, g, m, pr, hh: mm(out, lhs[:, g, hh, :], rhs[:, g, hh, :], start=True, stop=True)

            rt, kt, bbar, kbar = e[0], e[1], e[2], e[5]
            heads("Auk", pairs(kbar, kt))
            heads("Brk", pairs(kbar, rt))
            heads("Aub", pairs(bbar, kt))
            heads("Brb", pairs(bbar, rt))
            heads("A8", pairs(kt, bbar))
            heads("A2", prod(aAT, aA), "A8", "Aub")
            heads("A2T", prod(aA, aAT))
            heads("X1T", prod(aI, aAT), "A2")
            heads("A4", prod(aA2T, aA2), "A2T")
            heads("X", prod(aA, aI), "X1T", "A4")
            heads("XT", prod(aI, aA))
            heads("LX", prod(aL1T, aA2), "X")
            heads("X2", prod(aA2T, aAT), "LX", "XT")
            heads("X2T", prod(aAT, aA2T))
            heads("LX2", prod(aL2T, aA), "X2")
            heads("MT", prod(aA2, aI), "LX2", "X2T")
            after(pe, "tV1", "tK1", "tC1", "tB1")
            head = lambda pr, hh: slice((2 * hh + pr) * 64, (2 * hh + pr) * 64 + 64)
            for g, (m, pr) in enumerate(GRP):
                job = f"AV{m}{pr}"
                give(job)
                for hh in range(4):
                    last = mm(psum(job, 4, 64)[:, hh, :], aAuk[:, g, hh, :], natV[:, m, head(pr, hh)], start=True, stop=True)
                done(last, job)

            def hg(out, g, m, pr, hh):
                mm(out[:, 0:64], aA2T[:, g, hh, :], natK[:, m, head(pr, hh)], start=True, stop=True)
                return mm(out[:, 64:128], aA2T[:, g, hh, :], AV[:, g, hh, :], start=True, stop=True)

            def y0(out, g, m, pr, hh):
                q = slice(pr * 64, pr * 64 + 64)
                mm(out[q], natV[:, m, head(pr, hh)], aBrk[:, g, hh, :], start=True, stop=False)
                return mm(out[q], HG[:, g, hh, 64:128], aBrb[:, g, hh, :], start=False, stop=True)

            def rp(out, g, m, pr, hh):
                q = slice(pr * 64, pr * 64 + 64)
                return mm(out[q], HG[:, g, hh, 0:64], aBrb[:, g, hh, :], start=True, stop=True)

            heads("HG", hg, "MT", "AV")
            heads("Y0", y0, "HG")
            heads("Rp", rp)
            for c in range(NCH):
                job = f"TZ{c}"
                give(job)
                m, r = c // 4, slice((c % 4) * CH, (c % 4) * CH + CH)
                p2 = psum(job, 2, 4, 64)
                for h in range(H):
                    pr, hh = h % 2, h // 2
                    g, q, hs = m * 2 + pr, slice(pr * 64, pr * 64 + 64), head(h % 2, h // 2)
                    if c:
                        mm(p2[q, 0, hh, :], HG[r, g, hh, 0:64], natB[r, m, hs], start=True, stop=True)
                    mm(p2[q, 1, hh, :], natC[r, m, hs], natV[r, m, hs], start=True, stop=False)
                    last = mm(p2[q, 1, hh, :], natB[r, m, hs], HG[r, g, hh, 64:128], start=False, stop=True)
                done(last, job)
            for c in range(1, NCH):
                job = f"st{c}"
                after(pe, f"TZ{c}")
                pe.wait_ge(S_("state"), c)
                give(job)
                for hh in range(4):
                    last = mm(psum(job, 4, 64)[:, hh, :], TT[:, c, hh, :], stc[c - 1][:, hh, :], start=True, stop=True)
                done(last, job)
            after(pe, "Rp10", "Rp11")
            for c in range(1, NCH):
                job = f"yt{c}"
                pe.wait_ge(S_("std"), c)
                give(job)
                d = STd[:, c - 1] if c - 1 < 4 else STe[:, c - 5]
                for hh in range(4):
                    last = mm(psum(job, 4, CH)[:, hh, :], d[:, hh, :], Rp[:, hh, c * CH:(c + 1) * CH], start=True, stop=True)
                done(last, job)
            pe.wait_ge(S_("state"), NCH)
            transposes("wkv", [stc[NCH - 1][:, hh, :] for hh in range(4)], 128, 64)
            pe.wait_ge(S_("ld_ysn"), 16)
            transposes("sy", [ysn[:NB, c * 128:(c + 1) * 128] for c in range(4)], NB)
            after(pe, "wkv", "sy")
            pe.sem_inc(S_("unit_used"), 4)
            for c in range(4):
                give(f"mu{c}")
                done(mm(psum(f"mu{c}", T), C["head_mean"], YT[:, c, :], start=True, stop=True), f"mu{c}")
            pe.wait_ge(S_("y_sq"), 1)
            for c in range(4):
                give(f"va{c}")
                done(mm(psum(f"va{c}", T), C["head_mean"], e4w[:, c, :], start=True, stop=True), f"va{c}")
            pe.wait_ge(S_("ld_wa"), 16)
            pe.wait_ge(S_("ld_wb"), 16)
            pe.wait_ge(S_("obT"), 1)
            for d in range(KD):
                for k, w, src in (("ma", wa, oaT), ("mb", wb, YT)):
                    give(f"{k}{d}")
                    for c in range(4):
                        last = mm(psum(f"{k}{d}", T), w[:, c, d * 128:(d + 1) * 128], src[:, c, :], start=c == 0, stop=c == 3)
                    done(last, f"{k}{d}")
            after(pe, "ma7", "mb7")
            pe.sem_inc(S_("unit_used"), 4)
            pe.wait_ge(S_("ld_wo"), 16)
            pe.wait_ge(S_("mix"), KD)
            for m in range(NM):
                for g in range(2):
                    job = f"wo{m}{g}"
                    give(job)
                    for k in range(KD):
                        last = mm(psum(job, 512, parts=ROWS[m]), mixT[:, k, m * 128:m * 128 + ROWS[m]],
                                  wo[:, k, g * 512:(g + 1) * 512], start=k == 0, stop=k == KD - 1)
                    done(last, job)
            after(pe, "wo20", "wo21")
            pe.sem_inc(S_("unit_used"), 4)
            for m in range(NM):
                pe.wait_ge(S_("h2"), m + 1)
                for g in range(2):
                    transposes(f"ht{m}{g}", [h2[:ROWS[m], m, (4 * g + c) * 128:(4 * g + c + 1) * 128] for c in range(4)], ROWS[m])
            after(pe, "ht20", "ht21")
            pe.wait_ge(S_("ld_router"), 48)
            give("lg")
            for m in range(NM):
                n = ROWS[m]
                for k in range(KD):
                    last = mm(psum("lg", NM, NE)[:n, m, :], h2T[:, k, m * 128:m * 128 + n], wr[:, k, :], start=k == 0, stop=k == KD - 1)
            done(last, "lg")
            pe.wait_ge(S_("sel_r"), 1)
            give("rk")
            for m in range(4):
                for mp in range(m if m < 3 else 3):
                    mm(psum("rk", 4, NE)[:, m, :], C["ones"], selr[:, mp, :], start=mp == 0, stop=(m == 3 and mp == 2))
                if m < 3:
                    mm(psum("rk", 4, NE)[:, m, :], C["before"], selr[:, m, :], start=m == 0, stop=True)
            last = mm(psum("rk", 4, NE)[:, 3, :], C["ones"], selr[:, 0, :], start=True, stop=False)
            mm(psum("rk", 4, NE)[:, 3, :], C["ones"], selr[:, 1, :], start=False, stop=False)
            done(mm(psum("rk", 4, NE)[:, 3, :], C["ones"], selr[:, 2, :], start=False, stop=True), "rk")
            pe.wait_ge(S_("gate"), 3)
            transposes("gT", [gate[:, m, :] for m in range(NM)], 128, NE)
            after(pe, "gT")
            for m in range(NM):
                for g in range(2):
                    job = f"bd{m}{g}"
                    give(job)
                    done(mm(psum(job, 512, parts=ROWS[m]), gateT[:NE, m, :ROWS[m]], bdn[:NE, g * 512:(g + 1) * 512], start=True, stop=True), job)

            for b in range(8):
                last_of = max(turn[j] for j in jobs if bank[j] == b)
                pe.wait_ge(evac[b], last_of)

            def gather(it, sem_name, count):
                pe.wait_ge(S_(sem_name), count)
                for m in range(NM):
                    for g in range(2):
                        last = mm(PS[0][g * 64:g * 64 + 64, :], sel[:, m, :], h2[:, m, g * 512:(g + 1) * 512],
                                  start=m == 0, stop=m == NM - 1)
                last.then_inc(S_("xg_full"), 1)

            def gather_T(it):
                pe.wait_ge(S_("xg_out"), it + 1)
                for c in range(4):
                    last = nc.tensor.transpose(PS[1][:, c * 128:(c + 1) * 128], xg[:, c * 128:(c + 1) * 128], C["ident"])
                last.then_inc(S_("xgT_full"), 1)

            def combine(it):
                pe.wait_ge(S_("selgT_out"), it + 1)
                pe.wait_ge(S_("y_out"), it + 1)
                pe.wait_ge(S_("acc_done"), it * 6 + 2)
                for m in range(NM):
                    for g in range(2):
                        q = slice(g * 64, g * 64 + 64)
                        last = mm(PS[CMB[m][g]][:, :], selgT[q, m * 128:(m + 1) * 128], yS[q, :], start=True, stop=True)
                    last.then_inc(S_("cmb_full"), 1)

            pe.wait_ge(S_("npass"), 1)
            pe.wait_ge(S_("moe_zero"), 1)
            passes = pe.value_load(npass[0:1, 0:1], min_val=1, max_val=PASSES)
            gather(0, "sel", 1)
            gather_T(0)
            with pe.Fori(0, passes) as p:
                with pe.Fori(0, NE) as ex:
                    it = pe.snap(p * NE + ex)
                    pe.wait_ge(S_("xgT_out"), it + 1)
                    for k in range(KD):
                        pe.wait_ge(S_(f"ld_u{k}"), it * 16 + 16)
                        h_, c_ = k // 4, k % 4
                        lhs = xgT[:, c_, h_ * 64:h_ * 64 + 64]
                        for bnk, base in ((2, 0), (3, 1024)):
                            for g in range(2):
                                last = mm(PS[bnk][g * 64:g * 64 + 64, :], lhs,
                                          UNIT[k][:, base + g * 512:base + (g + 1) * 512], start=k == 0, stop=False)
                        last.then_inc(S_("unit_used"), 1)
                    pe.wait_ge(S_("ld_b"), it * 16 + 16)
                    for bnk, base in ((2, 0), (3, 1024)):
                        for g in range(2):
                            last = mm(PS[bnk][g * 64:g * 64 + 64, :], C["ones"][:, 0:64],
                                      brow[:, base + g * 512:base + (g + 1) * 512], start=False, stop=True)
                    last.then_inc(S_("gu_full"), 1)
                    combine(it)
                    pe.wait_ge(S_("acc_done"), it * 6 + 4)
                    gather(it, "sel_next", it * 3 + 3)
                    pe.wait_ge(S_("selg"), it * 3 + 3)
                    pe.wait_ge(S_("acc_done"), it * 6 + 8)
                    for m in range(NM):
                        last = nc.tensor.transpose(PS[5][:, m * 128:(m + 1) * 128], selg[:, m, :], C["ident"])
                    last.then_inc(S_("selgT_full"), 1)
                    gather_T(it + 1)
                    pe.wait_ge(S_("act"), it + 1)
                    for c in range(4):
                        last = nc.tensor.transpose(PS[4][:, c * 128:(c + 1) * 128], up[:, c * 128:(c + 1) * 128], C["ident"])
                    last.then_inc(S_("actT_full"), 1)
                    pe.wait_ge(S_("actT_out"), it + 1)
                    pe.wait_ge(S_("selgT_out"), it + 2)
                    for k in range(KD):
                        u = KD + k // 2
                        if k % 2 == 0:
                            pe.wait_ge(S_(f"ld_u{u}"), it * 16 + 16)
                        h_, c_ = k // 4, k % 4
                        lhs = actT[:, c_, h_ * 64:h_ * 64 + 64]
                        for g in range(2):
                            w0 = (k % 2) * 1024 + g * 512
                            last = mm(PS[5][g * 64:g * 64 + 64, :], lhs, UNIT[u][:, w0:w0 + 512], start=k == 0, stop=k == KD - 1)
                        if k % 2:
                            last.then_inc(S_("unit_used"), 1)
            combine(pe.snap(passes * NE))


_INS = ["x_prompt", "x_sample", "cache_k", "cache_v", "state_wkv", "state_shift", "rel_bias", "ln1", "w_in", "rwkv_mu",
        "w0", "w_decay_up", "a0", "w_a_up", "w_g_up", "k_k", "k_a", "r_k", "gn_w", "gn_b", "w_branch_a", "w_branch_b",
        "w_out", "ln2", "w_router", "b_router", "w_gate_up", "b_gate_up", "w_down", "b_down", "ln_f"]
_OUTS = [("yp", (1, S, D)), ("ys", (NB, 1, D)), ("pk", (1, 1, S, H, E64)), ("pv", (1, 1, S, H, E64)),
         ("pwkv", (1, 1, H, E64, E64)), ("pshift", (1, 1, RC)), ("sk", (1, NB, 1, H, E64)), ("sv", (1, NB, 1, H, E64)),
         ("swkv", (1, NB, H, E64, E64)), ("sshift", (1, NB, RC))]


def kernel(**inputs):
    import concourse.bacc as bacc
    from concourse.bass_utils import run_bass_kernel_spmd

    nc = bacc.Bacc("TRN2", target_bir_lowering=False, num_devices=1)
    arrays = {f"in_{n}": np.ascontiguousarray(inputs[n]) for n in _INS}
    arrays.update({f"in_{n}": a for n, a in shape_constants().items()})
    A = {n[3:]: nc.dram_tensor(n, a.shape, mybir.dt.from_np(a.dtype), kind="ExternalInput").ap() for n, a in arrays.items()}
    O = {n: nc.dram_tensor(f"out_{n}", shape, F32, kind="ExternalOutput").ap() for n, shape in _OUTS}
    build(nc, A, O)
    r = run_bass_kernel_spmd(nc, [arrays], core_ids=[0])
    return tuple(r.results[0][f"out_{n}"] for n, _ in _OUTS)
```

```python
import concourse.bass as bass
from concourse import mybir
from contextlib import ExitStack
import numpy as np

F32 = mybir.dt.float32
I32 = mybir.dt.int32
ALU = mybir.AluOpType
ACT = mybir.ActivationFunctionType
AX = mybir.AxisListType

D = 1024
S = 256
NB = 8
T = S + NB
ROWS = [128, 128, NB]
NM = len(ROWS)
KD = D // 128
H = 8
E64 = 64
CA, CR, CG = 12, 14, 16
RC = CR * 128
SCALE = E64 ** -0.5
DECAY = float(np.exp(-0.5))
CH = 32
NCH = S // CH
NE = 32
FE = 1024
SLOT = 64
PASSES = -(-T // SLOT)
LIMIT, ALPHA = 7.0, 1.702
NEG = -1e30
BIG = 3e38
NREL = 383
KT = [128, 96, 97]
KO = [0, 128, 224]
NKEY = 321

P_LN1, P_MU, P_W0, P_A0, P_KK, P_KA, P_RK, P_GW, P_GB, P_N = 0, 8, 22, 26, 30, 34, 38, 42, 46, 50
CONST_NAMES = ["ident", "ones", "head_sum", "head_mean", "lo8", "up8", "up16", "up32", "strict", "incl",
               "neg_incl", "before", "slots", "idstack", "quad"]


def shape_constants():
    p = np.arange(128)[:, None]
    c = np.arange(128)[None, :]
    same = lambda n: p // n == c // n
    m = {
        "ident": p == c, "ones": p >= 0 * c, "head_sum": same(64), "head_mean": same(64) / 64.0,
        "lo8": same(8) & (c < p), "up8": same(8) & (p < c), "up16": same(16) & ~same(8) & (p < c),
        "up32": same(32) & ~same(16) & (p < c), "strict": same(32) & (p < c), "incl": same(32) & (p <= c),
        "neg_incl": -1.0 * (same(32) & (p <= c)), "before": p < c, "slots": 0 * p + c % SLOT + 1,
        "idstack": (p % 64 == c) & (c < 64), "quad": (p // 32 == c) & (c < 4),
    }
    mats = np.concatenate([(np.ones((128, 128)) * m[n]).astype(np.float32) for n in CONST_NAMES], axis=1)

    def bucket(d):
        d = np.asarray(d)
        f = np.maximum(d, 1).astype(np.float32)
        large = 16 + (np.log(f / np.float32(16)) / np.float32(np.log(2048 / 16)) * np.float32(16)).astype(np.int32)
        return np.where(d < 16, d, np.minimum(large, 31))

    def count(d):
        return (1 * (d <= 128) + 1 * ((d % 4 == 0) & (d <= 512)) + 1 * ((d % 16 == 0) & (d <= 2048))) * (d >= 0)

    dist_p = 255 - np.arange(NREL)
    dist_s = np.concatenate([128 - np.arange(128), 512 - 4 * np.arange(96), 2048 - 16 * np.arange(96), [0]])
    out = []
    for dist, rows in ((dist_p, H), (dist_s, NB * H)):
        hot = (np.arange(32)[:, None] == bucket(np.maximum(dist, 0))[None, :]).astype(np.float32)
        n = count(dist)
        log = np.where(n > 0, np.log(np.maximum(n, 1).astype(np.float32)), np.float32(NEG)).astype(np.float32)
        out += [hot, np.ascontiguousarray(np.broadcast_to(log, (rows, len(dist))))]
    return {"c_mats": mats, "c_hot_p": out[0], "c_log_p": out[1], "c_hot_s": out[2], "c_log_s": out[3],
            "c_own": (np.arange(128)[:, None] % 32 == np.arange(512)[None, :] // 64).astype(np.float32)}


def psum_jobs():
    jobs = ["par", "ssT"] + [f"hT{m}{g}" for m in range(NM) for g in range(2)]
    pr = lambda *groups: [f"pr{g * GC + j}" for g in groups for j in range(GC)]
    jobs += pr(2, 3, 4) + ["bvp", "bvs"] + [f"sh{g}" for g in range(4)] + pr(0)
    jobs += [f"lw{c}" for c in range(4)] + [f"la{c}" for c in range(4)] + [f"lg{c}" for c in range(4)] + pr(1)
    jobs += [f"nk{c}" for c in range(4)] + ["qn"] + [f"kn{m}" for m in range(NM)] + pr(5)
    jobs += pr(6) + [f"vn{m}" for m in range(NM)] + ["s0", "s1"]
    for h in range(H):
        jobs += [f"s{h + 2}"] * (h + 2 < H) + [f"pt{h}"] + [f"ov{h // 2}"] * (h % 2) + [f"sx{h}"] * (h < 6)
        jobs += [f"bo{h - 4}"] * (h >= 4) + ["sst"] * (h == 3) + ["spt"] * (h == 6) + ["pv0"] * (h == 7)
    jobs += ["pv1"]
    jobs += ["sv"]
    jobs += [f"{k}{m}" for m in range(2) for k in ("tV", "tK", "tC", "tB")]
    grp = [(m, par) for m in range(2) for par in range(2)]
    for k in ("Auk", "Brk", "Aub", "Brb", "A8", "A2", "A2T", "X1T", "A4", "X", "XT", "LX", "X2", "X2T", "LX2",
              "MT", "AV", "HG", "Y0", "Rp"):
        jobs += [f"{k}{m}{par}" for m, par in grp]
    jobs += STATE_JOBS
    jobs += [f"yt{c}" for c in range(1, NCH)] + ["wkv", "sy"]
    jobs += [f"mu{c}" for c in range(4)] + [f"va{c}" for c in range(4)]
    jobs += [f"mb{d}" for d in range(KD)]
    jobs += ["wo2", "wo00", "wo01", "ht20", "ht21", "wo10", "ht00", "ht01", "wo11", "ro2", "ro0", "ht10", "ht11", "ro1"]
    jobs += ["rk"]
    return jobs


STATE_JOBS = ["TZ0", "TZ1", "TZ2", "TZ3", "st1", "ma0", "st2", "ma1", "st3", "ma2",
              "TZ4", "TZ5", "TZ6", "TZ7", "ma3", "ma4", "st4", "ma5", "st5", "ma6", "st6", "ma7", "st7"]
MORDER = (2, 0, 1)
CMB = [(0, 1), (6, 7), (4, 5)]
GROUPS = [2, 3, 4, 0, 1, 5, 6]
GC = 6


def build(nc, A, O):
    jobs = psum_jobs()
    assert len(set(jobs)) == len(jobs)
    bank = {j: n % 8 for n, j in enumerate(jobs)}
    turn = {j: n // 8 + 1 for n, j in enumerate(jobs)}

    with ExitStack() as ctx:
        def sb(name, n, dt=F32, parts=128):
            return ctx.enter_context(nc.sbuf_tensor(name, [parts, n], dt))

        def sem(name):
            return ctx.enter_context(nc.semaphore(name))

        RING = sb("ring", 24576)
        WORK = sb("work", 28600)
        PS = [ctx.enter_context(nc.psum_tensor(f"ps{b}", [128, 512], F32)) for b in range(8)]

        def view(base, off, *dims):
            n = int(np.prod(dims))
            v = base[:, off:off + n]
            if len(dims) > 1:
                names = "abcd"[:len(dims)]
                v = v.rearrange("p (" + " ".join(names) + ") -> p " + " ".join(names),
                                **{k: d for k, d in zip(names[1:], dims[1:])})
            return v

        def bc(ap, at, n):
            ap = ap.unsqueeze(at)
            shape = list(ap.shape)
            shape[at] = n
            return ap.broadcast_to(shape)

        mats = view(WORK, 0, len(CONST_NAMES), 128)
        C = {n: mats[:, i, :] for i, n in enumerate(CONST_NAMES)}
        sm = [128 * len(CONST_NAMES)]

        def small(*dims):
            v = view(WORK, sm[0], *dims)
            sm[0] += int(np.prod(dims))
            assert sm[0] <= 2792
            return v

        par = small(128)
        parT = small(P_N)
        ssT = small(CR, NB)
        sq1 = small(3)
        rs1 = small(3)
        eps = small(1)
        gn_eps = small(1)
        sgs = small(4, NB)
        pcs = small(4, NCH)
        relb = small(H)
        relb64 = small(NB, H)
        svT = small(6, 4, NB)
        negm = small(H, 2)
        lsum = small(H, 2)
        rinv = small(H, 2)
        nms = small(1)
        lss = small(1)
        ris = small(1)
        ysm = small(2, 16)
        mcount = small(1)
        thr = small(PASSES)
        qkvT = view(WORK, 2792, CA, T)
        sgT = view(WORK, 5960, CG, T)
        rcT = view(WORK, 10184, CR, T)
        xr = view(WORK, 13880, CR, T)
        hT = view(WORK, 17576, KD, T)
        oaT = view(WORK, 19688, 4, T)
        wlora = view(WORK, 19688, 2, 512)
        e = [view(WORK, 20744 + 1024 * i, 4, S) for i in range(6)]
        kkn = view(WORK, 20744 + 6144, 4, T)
        spare = 20744 + 6144 + 1056
        ysn = view(WORK, spare, 512)
        aT = view(WORK, 10184, 4, T)
        gT_ = view(WORK, 10184 + 1056, 4, T)
        bT = view(WORK, 10184 + 2112, 4, T)
        scanX = view(WORK, 20744 + 4096, 4 * NCH, 2 * CH)
        Y0 = view(WORK, 17576, 4, S)
        Rp = view(WORK, 17576 + 1024, 4, S)
        svn = view(WORK, 17048, 5, 512)
        svn5 = view(WORK, 13352, 512)
        S1 = view(WORK, 2792, 16, E64)
        S1t = view(WORK, 2792 + 1024, 16, E64)
        svec = view(WORK, 2792 + 2048, 6, E64)
        u1 = view(WORK, 2792 + 2048 + 384, 16)
        mixT = view(WORK, 17576, KD, T)
        WIN = [view(RING, 6144 * i, KD, GC * 128) for i in range(2)]
        vn = view(RING, 0, NM, 512)
        ssb = view(RING, 1536, 2, 384)
        ptb = view(RING, 2304, 2, 384)
        qB = view(RING, 6144, NB, 512)
        own = view(RING, 11776, 512)
        Kb = [view(RING, 18432 + 1536 * i, 3, 512) for i in range(2)]
        kn = view(RING, 21504, NM, 512)
        PROD = [view(RING, 10240, 3, 512), view(RING, 23040, 3, 512)]
        Vb = [view(RING, 3072, 3, 512), view(RING, 4608, 3, 512), Kb[0], view(RING, 6144, 3, 512),
              view(RING, 7680, 3, 512), Kb[1], PROD[0], PROD[1]]
        B3 = view(RING, 12288, H, 384)
        shn = view(RING, 15360, RC)
        scanY = view(RING, 15360, 4 * NCH, 2 * CH)
        pts = view(RING, 15360, 3, NB, 32)
        pvm = view(RING, 15360 + 768, 2, 512)
        biasS = view(RING, 17408, NKEY)
        s64 = view(RING, 17729, NKEY)
        scs = view(RING, 18050, 3, 64)
        qn = view(RING, 17729, 512)
        X = view(RING, 18432, NM, D)
        XS = view(RING, 18432 + 3072, NM, D)
        bvec = view(WORK, spare, NREL)
        ss = view(WORK, 20744, RC)
        hot_p = view(WORK, 20744 + 1792, NREL)
        log_p = view(WORK, 20744 + 1792 + 383, NREL)
        hot_s = view(WORK, 20744 + 1792 + 766, NKEY)
        log_s = view(WORK, 20744 + 1792 + 766 + 321, NKEY)
        arr = [view(RING, 2048 * i, 4, 4, 128) for i in range(10)]
        natV = view(RING, 20480, 2, 512)
        natK = view(RING, 20480 + 1024, 2, 512)
        natC = view(RING, 20480 + 2048, 2, 512)
        natB = view(RING, 20480 + 3072, 2, 512)
        aA, aAT, aL1T, aL2T, aBrk, aBrb, aAuk, aA2, aA2T, aI = arr
        HG = aA2
        AV = view(RING, 2048 * 2, 4, 4, 64)
        TT = view(RING, 0, NCH, 4, 128)
        Zc = view(RING, 2048 * 2, NCH, 4, 64)
        STd = view(RING, 2048 * 3, 4, 4, 128)
        STe = view(RING, 2048 * 9, 4, 4, 128)
        stc = [view(RING, 2048 * 6 + 256 * i, 4, 64) for i in range(NCH)]
        wkvn = view(WORK, 20744 + 3072, 4, 128)
        wa = view(RING, 2048 * 4, 4, D)
        wb = view(RING, 2048 * 7, 4, D)
        wo = view(RING, 0, KD, D)

        YT = view(WORK, 20744 + 6144, 4, T)
        e4w = view(WORK, 20744 + 4096, 4, T)
        dtmp = view(WORK, 20744 + 1024, 4, 4, 64)
        UNIT = [view(RING, 2048 * u, 2048) for u in (6, 9, 10, 11, 4, 5, 7, 8, 0, 1, 2, 3)]
        acc = view(WORK, 2792, NM, D)
        brow = view(WORK, 5960, 2 * FE)
        wr = view(WORK, 8008, KD, NE)
        bdn = view(WORK, 8264, D)
        brow_r = view(WORK, 9288, NE)
        h2 = view(WORK, 10184, NM, D)
        ln2b = view(WORK, 13880, D)
        lnfb = view(WORK, 13880 + 1024, D)
        h2T = view(WORK, 17576, KD, T)
        mo = [19688]

        def moe_small(*dims):
            t = view(WORK, mo[0], *dims)
            mo[0] += int(np.prod(dims))
            return t

        posx = moe_small(NM, PASSES * NE + 1)
        gate = moe_small(NM, NE)
        selr = moe_small(NM, NE)
        lgt = moe_small(NM, NE + 4)
        rep = moe_small(NM, NE + 4)
        max8 = moe_small(NM, 8)
        ngm = moe_small(NM)
        gsum = moe_small(NM)
        assert mo[0] <= 20744
        mo[0] = 20744
        rexp = moe_small(NM, NE)
        sel = moe_small(NM, SLOT)
        selg = moe_small(NM, 128)
        xg = moe_small(512)
        xgT = moe_small(4, 128)
        gt = moe_small(512)
        up = moe_small(512)
        sg = moe_small(512)
        actT = moe_small(4, 128)
        yS = moe_small(512)
        selgT = moe_small(384)
        npass = sb("npass", 1, I32)
        full = [sem(f"bank{b}_full") for b in range(8)]
        evac = [sem(f"bank{b}_evacuated") for b in range(8)]
        SEM = {}

        def S_(name):
            if name not in SEM:
                SEM[name] = sem(name)
            return SEM[name]

        def take(eng, job):
            eng.wait_ge(full[bank[job]], turn[job])

        def after(eng, *names):
            for job in names:
                eng.wait_ge(evac[bank[job]], turn[job])

        def psum(job, *dims, parts=128):
            return view(PS[bank[job]], 0, *dims)[:parts]

        class Chain:

            def __init__(self, eng, name):
                self.eng, self.sem, self.n = eng, S_(name), 0

            def __call__(self, ins):
                self.n += 1
                ins.then_inc(self.sem, 1)
                self.eng.wait_ge(self.sem, self.n)

            def free(self, ins, job):
                ins.then_inc(evac[bank[job]], 1)
                self.eng.wait_ge(evac[bank[job]], turn[job])

            def ready(self, ins, name, n=1):
                ins.then_inc(S_(name), 1)
                self.eng.wait_ge(S_(name), n)

        GRP = [(m, par_) for m in range(2) for par_ in range(2)]
        bvec_d = nc.dram_tensor("bias_rows", (H, 128, NREL), F32, kind="Internal").ap()
        qn_d = nc.dram_tensor("sample_q", (NB, 512), F32, kind="Internal").ap()
        sv_d = nc.dram_tensor("sample_vectors", (NB, 6, 512), F32, kind="Internal").ap()
        ys_d = nc.dram_tensor("sample_y", (2, NB * H, 32), F32, kind="Internal").ap()
        block = ctx.enter_context(nc.Block())

        @block.sync
        def _(sp):
            def load(dst, src, name):
                sp.dma_start(dst, src).then_inc(S_(name), 16)

            def wait_pe(job):
                sp.wait_ge(full[bank[job]], turn[job])

            for m in range(2):
                load(X[:, m, :], A["x_prompt"][0, m * 128:(m + 1) * 128, :], f"ld_x{m}")
            load(X[:NB, 2, :], A["x_sample"][:, 0, :], "ld_x2")
            load(C["ident"], A["c_mats"][:, 0:128], "ld_ident")
            def load_win(i, part=""):
                c0, n = {"": (0, 768), "a": (0, 384), "b": (384, 384)}[part]
                src = A["w_in"][0, :, GROUPS[i] * 768 + c0:GROUPS[i] * 768 + c0 + n].rearrange("(k p) n -> p k n", p=128)
                load(WIN[i % 2][:, :, c0:c0 + n], src, f"ld_win{i}{part}")

            load_win(0, "a")
            row = lambda name, n: A[name].rearrange("l (c p) -> (l c) p", p=128)
            for name, at, n in (("ln1", P_LN1, 8), ("rwkv_mu", P_MU, CR), ("w0", P_W0, 4), ("a0", P_A0, 4),
                                ("k_k", P_KK, 4), ("k_a", P_KA, 4), ("gn_w", P_GW, 4), ("gn_b", P_GB, 4)):
                load(par[at:at + n, :], row(name, n), "ld_par")
            load(par[P_RK:P_RK + 4, :], A["r_k"][0].rearrange("(c a) d -> c (a d)", a=2), "ld_par")
            load(ss[:NB, :], A["state_shift"][0], "ld_ss")
            load_win(0, "b")
            load(WORK[:, 128:128 * len(CONST_NAMES)], A["c_mats"][:, 128:], "ld_mats")
            load_win(1)
            load(wlora[0:64, 0, :], A["w_decay_up"][0], "ld_lora")
            load(wlora[64:128, 0, :], A["w_a_up"][0], "ld_lora")
            load(wlora[:, 1, :], A["w_g_up"][0], "ld_lora")
            load(relb[:32, :], A["rel_bias"], "ld_bias")
            load(hot_p[:32], A["c_hot_p"], "ld_bias")
            load(log_p[:H], A["c_log_p"], "ld_bias")
            load(hot_s[:32], A["c_hot_s"], "ld_bias")
            load(log_s[:64], A["c_log_s"], "ld_bias")
            for i in range(2, 7):
                wait_pe(f"pr{GROUPS[i - 2] * GC + GC - 1}")
                load_win(i)
            cuts = ((0, 128, 1920, 1), (1, 96, 1536, 4), (2, 96, 0, 16))

            def load_cached(dst, src, b, name):
                for t, n, first, step in cuts:
                    rows = src[0, b, first:first + step * (n - 1) + 1:step].rearrange("s h d -> s (h d)")
                    load(dst[:n, t, :], rows, name)

            def load_new(dst, new, b, name):
                load(dst[96:97, 2, :], new[b:b + 1, 2, :], name)

            def load_v(v):
                load_cached(Vb[v], A["cache_v"], v, f"ld_v{v}")
                load_new(Vb[v], vn, v, f"ld_v{v}")

            sp.wait_ge(S_("kv_zero"), 1)
            for b in range(2):
                load_cached(Kb[b], A["cache_k"], b, f"ld_k{b}")
            after(sp, "kn2")
            for b in range(2):
                load_new(Kb[b], kn, b, f"ld_k{b}")
            for m in range(2):
                sp.dma_start(O["pk"][0, 0, m * 128:(m + 1) * 128].rearrange("s h d -> s (h d)"), kn[:, m, :]).then_inc(S_("st_out"), 16)
            sp.dma_start(O["sk"][0, :, 0].rearrange("b h d -> b (h d)"), kn[:NB, 2, :]).then_inc(S_("st_out"), 16)
            for b in range(2, NB):
                sp.wait_ge(S_("pool_prod"), b - 1)
                load_cached(Kb[b % 2], A["cache_k"], b, f"ld_k{b % 2}")
                load_new(Kb[b % 2], kn, b, f"ld_k{b % 2}")
            after(sp, "vn2")
            load_v(0)
            load_v(1)
            for m in range(2):
                sp.dma_start(O["pv"][0, 0, m * 128:(m + 1) * 128].rearrange("s h d -> s (h d)"), vn[:, m, :]).then_inc(S_("st_out"), 16)
            sp.dma_start(O["sv"][0, :, 0].rearrange("b h d -> b (h d)"), vn[:NB, 2, :]).then_inc(S_("st_out"), 16)
            sp.wait_ge(S_("pool_prod"), NB - 1)
            load_v(2)
            sp.wait_ge(S_("pool_prod"), NB)
            for v in (3, 4, 5):
                load_v(v)
            for v in (6, 7):
                sp.wait_ge(S_("s_red"), v + 1)
                load_v(v)
            wait_pe("s7")
            sp.wait_ge(S_("st_sv"), 32)
            for vh in range(2):
                for b in range(NB):
                    p0 = vh * 64 + b * H
                    load(svec[p0:p0 + H], sv_d[b].rearrange("x (h d) -> h x d", h=H), "ld_svec")
            wait_pe("Rp11")
            load(wa, A["w_branch_a"][0].rearrange("(k p) n -> p k n", p=128), "ld_wa")
            wait_pe("TZ7")
            load(wb, A["w_branch_b"][0].rearrange("(k p) n -> p k n", p=128), "ld_wb")
            after(sp, "yt7")
            load(wo, A["w_out"][0].rearrange("(k p) n -> p k n", p=128), "ld_wo")
            sp.wait_ge(S_("ld_ysn"), 16)
            for m in range(2):
                load(acc[:, m, :], A["x_prompt"][0, m * 128:(m + 1) * 128, :], "ld_acc")
            load(acc[:NB, 2, :], A["x_sample"][:, 0, :], "ld_acc")
            sp.wait_ge(S_("obT"), 1)
            load(ln2b, A["ln2"].broadcast_to([128, D]), "ld_ln")
            load(lnfb, A["ln_f"].unsqueeze(0).broadcast_to([128, D]), "ld_ln")
            sp.wait_ge(S_("mix"), KD)
            load(wr, A["w_router"][0].rearrange("(k p) e -> p k e", p=128), "ld_router")
            load(brow_r, A["b_router"].broadcast_to([128, NE]), "ld_router")
            wgu = A["w_gate_up"][0]
            wdn = A["w_down"][0]

            def load_bias(ex, name):
                dst, src = {"ld_b": (brow, "b_gate_up"), "ld_bd": (bdn, "b_down")}[name]
                sp.dma_start(dst[0:1, :], A[src][0, bass.ds(ex, 1), :]).then_inc(S_(name), 16)

            def load_expert(ex, free, biases=True):
                for k in range(KD):
                    free(k + 1)
                    if k == 0 and biases:
                        load_bias(ex, "ld_b")
                    sp.dma_start(UNIT[k], wgu[bass.ds(ex, 1), k * 128:(k + 1) * 128, :].rearrange("a p n -> p (a n)")).then_inc(S_(f"ld_u{k}"), 16)
                for u in range(4):
                    free(KD + u + 1)
                    if u == 0 and biases:
                        load_bias(ex, "ld_bd")
                    sp.dma_start(UNIT[KD + u].rearrange("p (j n) -> p j n", j=2),
                                 wdn[bass.ds(ex, 1), u * 256:(u + 1) * 256, :].rearrange("a (j p) n -> p (a j) n", p=128))\
                      .then_inc(S_(f"ld_u{KD + u}"), 16)

            load_expert(0, lambda n: sp.wait_ge(S_("unit_used"), n), biases=False)
            sp.wait_ge(S_("brow_zero"), 1)
            load_bias(0, "ld_b")
            load_bias(0, "ld_bd")
            with sp.Fori(1, NE) as ex:
                load_expert(ex, lambda n: sp.wait_ge(S_("unit_used"), ex * 12 + n))
            sp.wait_ge(S_("npass"), 1)
            passes = sp.value_load(npass[0:1, 0:1], min_val=1, max_val=PASSES)
            with sp.If(passes > 1):
                with sp.Fori(1, passes) as p:
                    with sp.Fori(0, NE) as ex:
                        it = sp.snap(p * NE + ex)
                        load_expert(ex, lambda n: sp.wait_ge(S_("unit_used"), it * 12 + n))

        @block.scalar
        def _(act):
            A_ = Chain(act, "act_step")

            def evacuate(job, dst, src, func=ACT.Copy, **kw):
                take(act, job)
                A_.free(nc.scalar.activation(dst, src, func, **kw), job)

            act.wait_ge(S_("eps"), 1)
            for m in range(NM):
                n = ROWS[m]
                act.wait_ge(S_(f"ld_x{m}"), 16)
                A_.ready(nc.scalar.activation(XS[:n, m, :], X[:n, m, :], ACT.Square, accum_out=sq1[:n, m:m + 1]),
                         "sumsq", m + 1)
            for m in range(NM):
                n = ROWS[m]
                A_.ready(nc.scalar.activation(rs1[:n, m:m + 1], sq1[:n, m:m + 1], ACT.Sqrt, bias=eps[:n], scale=1.0 / D), "rms1", m + 1)
            evacuate("par", parT, psum("par", P_N))
            evacuate("ssT", ssT, psum("ssT", CR, NB))
            def project(*groups):
                for n in [g * GC + j for g in groups for j in range(GC)]:
                    job = f"pr{n}"
                    if n < CA:
                        evacuate(job, qkvT[:, n, :], psum(job, T))
                    elif n < CA + CR:
                        evacuate(job, rcT[:, n - CA, :], psum(job, T))
                    else:
                        evacuate(job, sgT[:, n - CA - CR, :], psum(job, T), ACT.Sigmoid)

            project(2, 3, 4, 0)
            act.wait_ge(S_("xr_ready"), 1)
            A_.ready(nc.scalar.activation(xr[0:64, 12, :], xr[0:64, 12, :], ACT.Tanh), "lora_in", 1)
            A_.ready(nc.scalar.activation(xr[:, 13, :], xr[:, 13, :], ACT.Sigmoid), "lora_in", 2)
            act.wait_ge(S_("scan_zero"), 1)
            for c in range(4):
                job = f"lw{c}"
                take(act, job)
                col = parT[:, P_W0 + c:P_W0 + c + 1]
                A_(nc.scalar.activation(sgs[:, c, :], psum(job, T)[:, S:T], ACT.Sigmoid, bias=col))
                dst = scanX[:, c * NCH:(c + 1) * NCH, CH:2 * CH]
                A_.free(nc.scalar.activation(dst, psum(job, T)[:, 0:S].rearrange("p (a b) -> p a b", b=CH),
                                             ACT.Sigmoid, bias=col), job)
            for c in range(4):
                evacuate(f"la{c}", aT[:, c, :], psum(f"la{c}", T), ACT.Sigmoid, bias=parT[:, P_A0 + c:P_A0 + c + 1])
            for c in range(4):
                evacuate(f"lg{c}", gT_[:, c, :], psum(f"lg{c}", T))
            project(1)
            act.wait_ge(S_("kk_max"), 1)
            A_.ready(nc.scalar.activation(bT, bT, ACT.Sqrt), "kk_norm", 1)
            act.wait_ge(S_("scan_done"), 1)
            cur = scanY[:, :, CH:2 * CH]
            prv = scanY[:, :, CH - 1:2 * CH - 1]
            r3 = lambda t: t.rearrange("p c (n b) -> p (c n) b", b=CH)
            A_.ready(nc.scalar.activation(r3(e[0]), cur, ACT.Exp, scale=-DECAY), "decays", 1)
            A_.ready(nc.scalar.activation(r3(e[1]), prv, ACT.Exp, scale=-DECAY), "decays", 2)
            A_.ready(nc.scalar.activation(r3(e[2]), cur, ACT.Exp, scale=DECAY), "decays", 3)
            act.wait_ge(S_("rest_sum"), 1)
            A_.ready(nc.scalar.activation(e[3], e[3], ACT.Exp, scale=-DECAY), "decays", 4)
            A_.ready(nc.scalar.activation(svT[:, 0], sgs, ACT.Exp, scale=-DECAY), "decays", 5)

            evacuate("qn", qn[:NB, :], psum("qn", 512, parts=NB))
            act.dma_start(qn_d, qn[:NB, :]).then_inc(S_("st_qn"), 16)
            for m in range(NM):
                evacuate(f"kn{m}", kn[:ROWS[m], m, :], psum(f"kn{m}", 512, parts=ROWS[m]))
            project(5)
            act.wait_ge(S_("st_qn"), 16)
            for i in range(NB // 2):
                act.dma_start(qB[:, 2 * i:2 * i + 2], qn_d[2 * i:2 * i + 2].unsqueeze(0).broadcast_to([128, 2, 512])).then_inc(S_(f"ld_qB{i}"), 16)
            act.dma_start(own, A["c_own"]).then_inc(S_("ld_own"), 16)
            project(6)
            for m in range(NM):
                evacuate(f"vn{m}", vn[:ROWS[m], m, :], psum(f"vn{m}", 512, parts=ROWS[m]))
            def exponents(h):
                act.wait_ge(S_("scores"), h + 1)
                for t, (c0, c1) in enumerate(((0, 128), (128, 384))):
                    v = ssb[:, h % 2, c0:c1]
                    ins = nc.scalar.activation(v, v, ACT.Exp, bias=negm[:, h, t:t + 1], accum_out=lsum[:, h, t:t + 1])
                    A_.ready(ins, "probs", 2 * h + t + 1)

            exponents(0)
            for h in range(H):
                if h + 1 < H:
                    exponents(h + 1)
                if h >= 2:
                    take(act, f"ov{h // 2 - 1}")
                evacuate(f"pt{h}", ptb[:, h % 2, :], psum(f"pt{h}", 384))
                if h < 6:
                    evacuate(f"sx{h}", svn[:NB, h, :] if h < 5 else svn5[:NB], psum(f"sx{h}", 512, parts=NB))
                if h == 4:
                    act.wait_ge(S_("s_scores"), 1)
                    A_.ready(nc.scalar.activation(s64[:64], s64[:64], ACT.Exp, bias=nms[:64], accum_out=lss[:64]), "s_probs", 1)
                if h == 6:
                    act.wait_ge(S_("pts_zero"), 1)
                    take(act, "spt")
                    for t in range(3):
                        ins = nc.scalar.activation(pts[:KT[t], t, :, 0:H], psum("spt", 3, NB, H)[:KT[t], t], ACT.Copy)
                        A_.free(ins, "spt") if t == 2 else A_(ins)
            act.dma_start(sv_d[:, 0:5], svn[:NB]).then_inc(S_("st_sv"), 16)
            act.dma_start(sv_d[:, 5], svn5[:NB]).then_inc(S_("st_sv"), 16)
            act.wait_ge(S_("st_out"), 16 * 6)
            for m in range(2):
                evacuate(f"tV{m}", natV[:, m, :], psum(f"tV{m}", 512))
                evacuate(f"tK{m}", natK[:, m, :], psum(f"tK{m}", 512))
            for g, (m, pr) in enumerate(GRP):
                take(act, f"A2{m}{pr}")
                A_.ready(nc.scalar.activation(aA2[:, g], psum(f"A2{m}{pr}", 4, 128), ACT.Copy), "square_copied", g + 1)
            for k, dst in (("A2T", aA2T), ("LX", aAT), ("LX2", aA2), ("AV", None), ("HG", None)):
                for g, (m, pr) in enumerate(GRP):
                    job = f"{k}{m}{pr}"
                    if k == "AV":
                        evacuate(job, AV[:, g], psum(job, 4, 64))
                    elif k == "HG":
                        evacuate(job, HG[:, g], psum(job, 4, 128))
                    else:
                        evacuate(job, dst[:, g], psum(job, 4, 128))
            def diagonal(c):
                after(act, f"st{c}") if c else act.wait_ge(S_("state"), 1)
                d = STd[:, c] if c < 4 else STe[:, c - 4]
                A_(nc.scalar.activation(d[0:64, :, 0:64], stc[c][0:64], ACT.Copy))
                A_.ready(nc.scalar.activation(d[64:128, :, 64:128], stc[c][64:128], ACT.Copy), "std", c + 1)

            def chunk_inputs(m):
                for c in range(4 * m, 4 * m + 4):
                    take(act, f"TZ{c}")
                    A_.ready(nc.scalar.activation(Zc[:, c], psum(f"TZ{c}", 2, 4, 64)[:, 1], ACT.Copy), "z_out", c + 1)

            chunk_inputs(0)
            act.wait_ge(S_("std_zero"), 2)
            for c in range(4):
                diagonal(c)
            chunk_inputs(1)
            for c in range(4, NCH - 1):
                diagonal(c)
            evacuate("wkv", wkvn[:64], psum("wkv", 4, 128, parts=64))
            act.dma_start(O["pwkv"][0, 0].rearrange("(c a) v k -> v c a k", a=2),
                          wkvn[:64].rearrange("p c (a k) -> p c a k", a=2)).then_inc(S_("st_wkv"), 16)
            for c in range(4):
                after(act, f"mu{c}")
                A_.ready(nc.scalar.activation(e4w[:, c, :], YT[:, c, :], ACT.Square), "y_sq", c + 1)
            for c in range(4):
                evacuate(f"va{c}", e4w[:, c, :], psum(f"va{c}", T), ACT.Sqrt, bias=gn_eps)

            def rms2(i):
                m = MORDER[i]
                n = ROWS[m]
                after(act, "wo2" if m == 2 else f"wo{m}1")
                A_(nc.scalar.activation(h2[:n, m, :], acc[:n, m, :], ACT.Square, accum_out=sq1[:n, m:m + 1]))
                A_.ready(nc.scalar.activation(rs1[:n, m:m + 1], sq1[:n, m:m + 1], ACT.Sqrt, bias=eps[:n], scale=1.0 / D), "rms2", i + 1)

            def h2_T(m):
                for g in range(2):
                    evacuate(f"ht{m}{g}", h2T[:, 4 * g:4 * g + 4, m * 128:m * 128 + ROWS[m]], psum(f"ht{m}{g}", 4, ROWS[m]))

            rms2(0)
            rms2(1)
            h2_T(2)
            h2_T(0)
            rms2(2)
            h2_T(1)
            act.wait_ge(S_("st_wkv"), 16)
            for i, m in enumerate(MORDER):
                n = ROWS[m]
                act.wait_ge(S_("sel_r"), i + 1)
                A_.ready(nc.scalar.activation(rexp[:n, m, :], lgt[:n, m, 0:NE], ACT.Exp, bias=ngm[:n, m:m + 1]), "r_exp", i + 1)

            def gathered(it):
                act.wait_ge(S_("xg_full"), it + 1)
                nc.scalar.activation(xg, PS[0][:, :], ACT.Copy).then_inc(S_("xg_out"), 1)

            def gathered_T(it):
                act.wait_ge(S_("xgT_full"), it + 1)
                nc.scalar.activation(xgT, PS[1][:, :].rearrange("p (c s) -> p c s", c=4), ACT.Copy).then_inc(S_("xgT_out"), 1)

            gathered(0)
            gathered_T(0)
            act.wait_ge(S_("moe_zero"), 1)
            act.wait_ge(S_("npass"), 1)
            nc.scalar.activation(lss[:1], lss[:1], ACT.Copy).then_inc(S_("y_out"), 1)
            act.wait_ge(S_("y_out"), 1)
            nc.scalar.activation(lss[:1], lss[:1], ACT.Copy).then_inc(S_("selgT_out"), 1)
            passes = act.value_load(npass[0:1, 0:1], min_val=1, max_val=PASSES)
            with act.Fori(0, passes) as p:
                with act.Fori(0, NE) as ex:
                    it = act.snap(p * NE + ex)
                    act.wait_ge(S_("gt"), it + 1)
                    nc.scalar.activation(sg, gt, ACT.Sigmoid, scale=ALPHA).then_inc(S_("sg"), 1)
                    gathered(it + 1)
                    act.wait_ge(S_("selgT_full"), it + 1)
                    nc.scalar.activation(selgT, PS[5][:, 0:384], ACT.Copy).then_inc(S_("selgT_out"), 1)
                    gathered_T(it + 1)
                    act.wait_ge(S_("actT_full"), it + 1)
                    nc.scalar.activation(actT, PS[4][:, :].rearrange("p (c s) -> p c s", c=4), ACT.Copy).then_inc(S_("actT_out"), 1)
                    act.wait_ge(S_("unit_used"), it * 12 + 24)
                    nc.scalar.activation(yS, PS[5][:, :], ACT.Copy).then_inc(S_("y_out"), 1)
            last = act.snap(passes * NE)
            for m in range(NM):
                n = ROWS[m]
                act.wait_ge(S_("acc_done"), last * 6 + (2 * m + 4))
                A_(nc.scalar.activation(h2[:n, m, :], acc[:n, m, :], ACT.Square, accum_out=sq1[:n, m:m + 1]))
                A_.ready(nc.scalar.activation(rs1[:n, m:m + 1], sq1[:n, m:m + 1], ACT.Sqrt, bias=eps[:n], scale=1.0 / D), "rms3", m + 1)
            for m in range(NM):
                act.wait_ge(S_("y"), m + 1)
                dst = O["yp"][0, m * 128:(m + 1) * 128, :] if m < 2 else O["ys"][:, 0, :]
                act.dma_start(dst, acc[:ROWS[m], m, :]).then_inc(S_("st_y"), 16)
            act.wait_ge(S_("st_y"), 48)

        @block.gpsimd
        def _(pool):
            G_ = Chain(pool, "pool_step")
            pool.wait_ge(S_("ld_bias"), 16 * 5)
            G_.ready(nc.gpsimd.tensor_copy(relb64[:32], bc(relb[:32], 1, NB)), "relb64", 1)
            pool.wait_ge(S_("bvec"), 1)
            pool.dma_start(bvec_d, bc(bvec[:H], 1, 128)).then_inc(S_("st_bv"), 16)
            pool.wait_ge(S_("st_bv"), 16)
            pool.dma_start(B3[:, :, 128:384], bass.AP(bvec_d.tensor, 127, [[NREL - 1, 128], [128 * NREL, H], [1, 256]])).then_inc(S_("ld_B3"), 16)
            pool.dma_start(B3[:, :, 0:128], bass.AP(bvec_d.tensor, 255, [[NREL - 1, 128], [128 * NREL, H], [1, 128]])).then_inc(S_("ld_B3"), 16)
            pool.wait_ge(S_("shn"), 1)
            pool.dma_start(O["pshift"][0], shn[0:1, :]).then_inc(S_("st_sh"), 16)
            pool.dma_start(O["sshift"][0], shn[1:9, :]).then_inc(S_("st_sh"), 16)
            for b in range(NB):
                if b % 2 == 0:
                    pool.wait_ge(S_(f"ld_qB{b // 2}"), 16)
                pool.wait_ge(S_(f"ld_k{b % 2}"), 64 * (b // 2 + 1))
                if b >= 2:
                    pool.wait_ge(S_("s_red"), b - 1)
                G_.ready(nc.gpsimd.tensor_tensor(PROD[b % 2], Kb[b % 2],
                                                 bc(qB[:, b, :], 1, 3), ALU.mult), "pool_prod", b + 1)
            sw = A["state_wkv"][0].rearrange("b h v k -> (b h) v k")
            ow = O["swkv"][0].rearrange("b h v k -> (b h) v k")
            pool.wait_ge(full[bank["s7"]], turn["s7"])
            over_v = lambda t: bc(t, 1, 16)
            over_k = lambda t: bc(t, 2, E64)
            vw, vk, vb_, vkr, vv, vr_ = range(6)
            for q in range(2):
                for vh in range(2):
                    v0 = vh * 32 + q * 16
                    pool.dma_start(S1[vh * 64:vh * 64 + 64], sw[:, v0:v0 + 16, :]).then_inc(S_("ld_S"), 16)
                pool.wait_ge(S_("ld_S"), 32 * (q + 1))
                pool.wait_ge(S_("ld_svec"), 16 * 16)
                tt = nc.gpsimd.tensor_tensor
                G_(tt(S1t, S1, over_v(svec[:, vk]), ALU.mult))
                G_.ready(nc.gpsimd.tensor_tensor(S1, S1, over_v(svec[:, vw]), ALU.mult), "s_t1", q + 1)
                pool.wait_ge(S_("s_u1"), q + 1)
                G_(tt(S1t, over_k(u1), over_v(svec[:, vb_]), ALU.mult))
                G_(tt(S1, S1, S1t, ALU.subtract))
                for vh in range(2):
                    ps_ = slice(vh * 64, vh * 64 + 64)
                    v0 = vh * 32 + q * 16
                    G_(tt(S1t[ps_], over_k(svec[ps_, vv, v0:v0 + 16]), over_v(svec[ps_, vkr]), ALU.mult))
                G_(tt(S1, S1, S1t, ALU.add))
                for vh in range(2):
                    v0 = vh * 32 + q * 16
                    pool.dma_start(ow[:, v0:v0 + 16, :], S1[vh * 64:vh * 64 + 64]).then_inc(S_("st_S"), 16)
                G_.ready(tt(S1t, S1, over_v(svec[:, vr_]), ALU.mult), "s_t2", q + 1)
                pool.wait_ge(S_("s_y"), q + 1)
                pool.wait_ge(S_("st_S"), 32 * (q + 1))
            pool.dma_start(ys_d.rearrange("a r v -> (a r) v"), ysm.rearrange("p a b -> p (a b)")).then_inc(S_("st_ys"), 16)
            pool.wait_ge(S_("st_ys"), 16)
            pool.dma_start(ysn[:NB].rearrange("b (h a v) -> b h a v", h=H, a=2),
                           ys_d.rearrange("a (b h) v -> b h a v", b=NB)).then_inc(S_("ld_ysn"), 16)
            pool.wait_ge(S_("st_sh"), 32)

        @block.vector
        def _(dve):
            V = Chain(dve, "dve_step")
            v = nc.vector

            def tt(out, a, b, op):
                return v.tensor_tensor(out, a, b, op)

            def parc(at, n=4, width=T):
                return bc(parT[:, at:at + n], 2, width)

            V(v.memset(gn_eps, 64e-5))
            V.ready(v.memset(eps, 1e-6), "eps", 1)
            for m in range(NM):
                n = ROWS[m]
                dve.wait_ge(S_("rms1"), m + 1)
                V(v.reciprocal(rs1[:n, m:m + 1], rs1[:n, m:m + 1]))
                V.ready(v.tensor_scalar(XS[:n, m, :], X[:n, m, :], rs1[:n, m:m + 1], None, ALU.mult), "xs", m + 1)
            after(dve, "par")
            for m in range(NM):
                n = ROWS[m]
                for g in range(2):
                    job = f"hT{m}{g}"
                    take(dve, job)
                    V.free(tt(hT[:, g * 4:(g + 1) * 4, m * 128:m * 128 + n], psum(job, 4, n),
                              parc(P_LN1 + 4 * g, 4, n), ALU.mult), job)
            V(v.memset(RING[96:128, 18432:21504], 0.0))
            V.ready(v.memset(mcount, 0.0), "kv_zero", 1)
            after(dve, "ssT", *[f"pr{CA + c}" for c in range(CR)])
            V(tt(xr[:, :, 1:S], rcT[:, :, 0:S - 1], rcT[:, :, 1:S], ALU.subtract))
            V(v.tensor_scalar(xr[:, :, 0:1], rcT[:, :, 0:1], -1.0, None, ALU.mult))
            V(tt(xr[:, :, S:T], ssT, rcT[:, :, S:T], ALU.subtract))
            V(tt(xr, xr, parc(P_MU, CR), ALU.mult))
            V.ready(tt(xr, xr, rcT, ALU.add), "xr_ready", 1)
            take(dve, "bvp")
            V.free(tt(bvec[:H], psum("bvp", NREL, parts=H), log_p[:H], ALU.add), "bvp")
            take(dve, "bvs")
            V.free(tt(biasS[:64], psum("bvs", NKEY, parts=64), log_s[:64], ALU.add), "bvs")
            V.ready(v.memset(mcount, 0.0), "bvec", 1)
            for g in range(4):
                job, n = f"sh{g}", (4 if g < 3 else 2) * 128
                take(dve, job)
                V.free(v.tensor_copy(shn[:9, g * 512:g * 512 + n], psum(job, n, parts=9)), job)
            V.ready(v.memset(scanX[:, :, 0:CH], 0.0), "shn", 1)
            dve.wait_ge(S_("st_sh"), 32)
            V(v.memset(scanY[:, :, 0:CH], 0.0))
            V.ready(v.memset(mcount, 0.0), "scan_zero", 1)
            after(dve, *[f"lw{c}" for c in range(4)])
            src, dst = scanX, scanY
            for i, reach in enumerate((1, 2, 4, 8, 16)):
                ins = tt(dst[:, :, CH:2 * CH], src[:, :, CH:2 * CH], src[:, :, CH - reach:2 * CH - reach], ALU.add)
                V.ready(ins, "scan_done", 1) if i == 4 else V(ins)
                src, dst = dst, src
            r3 = lambda t: t.rearrange("p c (n b) -> p (c n) b", b=CH)
            V.ready(tt(r3(e[3]), scanY[:, :, 2 * CH - 1:2 * CH].broadcast_to([128, 4 * NCH, CH]),
                       scanY[:, :, CH:2 * CH], ALU.subtract), "rest_sum", 1)
            rT, kT, vT = xr[:, 0:4], xr[:, 4:8], xr[:, 8:12]
            V(tt(kkn, kT, parc(P_KK), ALU.mult))
            V.ready(tt(bT, kkn, kkn, ALU.mult), "kk_sq", 1)
            after(dve, *[f"la{c}" for c in range(4)])
            for c in range(4):
                take(dve, f"nk{c}")
                V.free(v.tensor_scalar(bT[:, c, :], psum(f"nk{c}", T), 1e-24, None, ALU.max), f"nk{c}")
            V.ready(v.memset(mcount, 0.0), "kk_max", 1)
            V(v.scalar_tensor_tensor(e4w, aT, -1.0, kT, ALU.add, ALU.mult))
            V(tt(e4w, e4w, parc(P_KA), ALU.mult))
            V(tt(kT, kT, e4w, ALU.add))
            dve.wait_ge(S_("kk_norm"), 1)
            V(v.reciprocal(bT, bT))
            V(tt(kkn, kkn, bT, ALU.mult))
            V(tt(bT, kkn, aT, ALU.mult))
            dve.wait_ge(S_("decays"), 5)
            for i, t in enumerate((kkn, bT, kT, vT, rT)):
                V(v.tensor_copy(svT[:, 1 + i], t[:, :, S:T]))
            V(v.tensor_copy(pcs, e[0][:, :, CH - 1:S:CH]))
            V(tt(e[1], kkn[:, :, 0:S], e[1], ALU.mult))
            V(tt(e[0], rT[:, :, 0:S], e[0], ALU.mult))
            V(tt(e[5], kT[:, :, 0:S], e[2], ALU.mult))
            V(tt(e[2], bT[:, :, 0:S], e[2], ALU.mult))
            V(tt(e[4], kT[:, :, 0:S], e[3], ALU.mult))
            V.ready(v.scalar_tensor_tensor(e[3], e[3], -1.0, bT[:, :, 0:S], ALU.mult, ALU.mult), "products", 1)
            V(tt(bT, rT, kT, ALU.mult))
            V.ready(tt(bT, bT, parc(P_RK), ALU.mult), "rk", 1)

            def score(h):
                take(dve, f"s{h}")
                if h >= 2:
                    take(dve, f"pt{h - 2}")
                w = ssb[:, h % 2, :]
                V.free(v.scalar_tensor_tensor(w, psum(f"s{h}", 384), SCALE, B3[:, h, :], ALU.mult, ALU.add), f"s{h}")
                V(v.tensor_reduce(negm[:, h, 0:1], w[:, 0:128], AX.X, ALU.max, negate=True))
                V.ready(v.tensor_reduce(negm[:, h, 1:2], w[:, 128:384], AX.X, ALU.max, negate=True), "scores", h + 1)

            def normalise(h):
                dve.wait_ge(S_("probs"), 2 * h + 2)
                V(v.reciprocal(rinv[:, h, :], lsum[:, h, :]))
                V(v.tensor_scalar(ssb[:, h % 2, 0:128], ssb[:, h % 2, 0:128], rinv[:, h, 0:1], None, ALU.mult))
                V.ready(v.tensor_scalar(ssb[:, h % 2, 128:384], ssb[:, h % 2, 128:384], rinv[:, h, 1:2], None, ALU.mult),
                        "pn", h + 1)

            def reduce_b(b):
                dve.wait_ge(S_("pool_prod"), b + 1)
                src = PROD[b % 2].rearrange("p t (h d) -> p t h d", h=H)
                V.ready(v.tensor_reduce(scs[:, :, b * H:(b + 1) * H], src, AX.X, ALU.add),
                        "s_red", b + 1)

            V.ready(v.memset(pts, 0.0), "pts_zero", 1)
            dve.wait_ge(S_("ld_B3"), 32)
            dve.wait_ge(S_("st_qn"), 16)
            for b in range(5):
                reduce_b(b)
            score(0)

            def own_columns(g):
                if g == 0:
                    dve.wait_ge(S_("ld_own"), 16)
                take(dve, f"pv{g}")
                V.free(tt(pvm[:, g, :], psum(f"pv{g}", 512), own, ALU.mult), f"pv{g}")

            def bonus(c):
                take(dve, f"bo{c}")
                V.free(tt(bT[:, c, :], psum(f"bo{c}", T), vT[:, c, :], ALU.mult), f"bo{c}")
                V(v.tensor_scalar(bT[:, c, :], bT[:, c, :], parT[:, P_GB + c:P_GB + c + 1], None, ALU.add))

            def attended(c):
                take(dve, f"ov{c}")
                V.free(v.tensor_copy(oaT[:, c, 0:S], psum(f"ov{c}", S)), f"ov{c}")

            for h in range(H):
                if h + 1 < H:
                    score(h + 1)
                normalise(h)
                if h >= 3 and h % 2:
                    attended(h // 2 - 1)
                if h >= 5:
                    bonus(h - 5)
                if h < 3:
                    reduce_b(5 + h)
                if h == 4:
                    take(dve, "sst")
                    V.free(v.scalar_tensor_tensor(s64[:64], psum("sst", NKEY, parts=64), SCALE, biasS[:64], ALU.mult, ALU.add), "sst")
                    V.ready(v.tensor_reduce(nms[:64], s64[:64], AX.X, ALU.max, negate=True), "s_scores", 1)
                if h == 5:
                    dve.wait_ge(S_("s_probs"), 1)
                    V(v.reciprocal(ris[:64], lss[:64]))
                    V.ready(v.tensor_scalar(s64[:64], s64[:64], ris[:64], None, ALU.mult), "s_pn", 1)
            attended(3)
            bonus(3)
            own_columns(0)
            own_columns(1)
            take(dve, "sv")
            V.free(v.tensor_copy(oaT[:, :, S:T], psum("sv", 4, NB)), "sv")
            for m in range(2):
                for k, dst in (("tC", natC), ("tB", natB)):
                    take(dve, f"{k}{m}")
                    V.free(v.tensor_copy(dst[:, m, :], psum(f"{k}{m}", 512)), f"{k}{m}")

            dve.wait_ge(S_("st_out"), 16 * 6)
            dve.wait_ge(S_("st_sh"), 32)
            def masked(kind, *pairs):
                for g, (m, pr) in enumerate(GRP):
                    job = f"{kind}{m}{pr}"
                    take(dve, job)
                    for n, (dst, mask) in enumerate(pairs):
                        ins = tt(dst[:, g], psum(job, 4, 128), bc(C[mask], 1, 4), ALU.mult)
                        V.free(ins, job) if n == len(pairs) - 1 else V(ins)

            masked("Auk", (aAuk, "strict"))
            masked("Brk", (aBrk, "incl"))
            masked("Aub", (aAT, "up8"), (aL1T, "up16"), (aL2T, "up32"))
            masked("Brb", (aBrb, "neg_incl"))
            masked("A8", (aA, "lo8"))

            def each(kind, fn):
                for g, (m, pr) in enumerate(GRP):
                    job = f"{kind}{m}{pr}"
                    take(dve, job)
                    V.free(fn(g, psum(job, 4, 128)), job)

            def sample_sum(kind, q):
                dve.wait_ge(S_("s_t1" if kind == "u" else "s_t2"), q + 1)
                if kind == "u":
                    V.ready(v.tensor_reduce(u1, S1t, AX.X, ALU.add), "s_u1", q + 1)
                else:
                    V.ready(v.tensor_reduce(ysm[:, q, :], S1t, AX.X, ALU.add), "s_y", q + 1)

            sample_sum("u", 0)
            for g, (m, pr) in enumerate(GRP):
                job = f"A2{m}{pr}"
                dve.wait_ge(S_("square_copied"), g + 1)
                V.free(tt(aI[:, g], psum(job, 4, 128), bc(C["ident"], 1, 4), ALU.add), job)
            for g, (m, pr) in enumerate(GRP):
                take(dve, f"A2T{m}{pr}")
                V.ready(tt(aAT[:, g], bc(C["ident"], 1, 4), aAT[:, g], ALU.subtract), "imat", g + 1)
            each("X1T", lambda g, p: v.tensor_copy(aA[:, g], p))
            each("A4", lambda g, p: tt(aI[:, g], p, bc(C["ident"], 1, 4), ALU.add))
            sample_sum("y", 0)
            each("X", lambda g, p: v.tensor_copy(aA2[:, g], p))
            each("XT", lambda g, p: v.tensor_copy(aA2T[:, g], p))
            sample_sum("u", 1)
            each("X2", lambda g, p: tt(aA[:, g], aA2[:, g], p, ALU.subtract))
            each("X2T", lambda g, p: tt(aI[:, g], aA2T[:, g], p, ALU.subtract))
            each("MT", lambda g, p: tt(aA2T[:, g], aI[:, g], p, ALU.subtract))
            V(v.memset(TT[0:64, :, :, 64:128], 0.0))
            V(v.memset(TT[64:128, :, :, 0:64], 0.0))
            sample_sum("y", 1)
            dve.wait_ge(S_("st_sv"), 32)
            for kind in ("Y0", "Rp"):
                for g, (m, pr) in enumerate(GRP):
                    job = f"{kind}{m}{pr}"
                    take(dve, job)
                    q = slice(pr * 64, pr * 64 + 64)
                    tok = slice(m * 128, m * 128 + 128)
                    if kind == "Y0":
                        V.free(v.tensor_copy(Y0[q, :, tok], psum(job, 4, 128)[q]), job)
                    else:
                        V.free(tt(Rp[q, :, tok], psum(job, 4, 128)[q], e[0][q, :, tok], ALU.add), job)
            V.ready(v.memset(STd, 0.0), "std_zero", 1)
            V.ready(v.memset(STe, 0.0), "std_zero", 2)
            def diagonals(m):
                for i in range(4):
                    V(tt(dtmp[:, i], bc(C["idstack"][:, 0:64], 1, 4),
                         pcs[:, :, 4 * m + i:4 * m + i + 1].broadcast_to([128, 4, 64]), ALU.mult))

            def transfer(c):
                job = f"TZ{c}"
                dve.wait_ge(S_("z_out"), c + 1)
                p2 = psum(job, 2, 4, 64)
                if c:
                    V(tt(TT[0:64, c, :, 0:64], p2[0:64, 0], dtmp[0:64, c % 4], ALU.add))
                    V.free(tt(TT[64:128, c, :, 64:128], p2[64:128, 0], dtmp[64:128, c % 4], ALU.add), job)
                else:
                    V.ready(v.tensor_copy(stc[0], Zc[:, 0]), "state", 1)
                    dve.sem_inc(evac[bank[job]], 1)

            def merge(k, n, d):
                take(dve, f"{k}{d}")
                w = sgT[:, n * KD + d, :]
                V.free(tt(w, psum(f"{k}{d}", T), w, ALU.mult), f"{k}{d}")

            diagonals(0)
            for job in STATE_JOBS:
                if job == "TZ4":
                    diagonals(1)
                c = int(job[2:])
                if job[:2] == "TZ":
                    transfer(c)
                elif job[:2] == "ma":
                    merge("ma", 0, c)
                else:
                    take(dve, job)
                    V.free(tt(stc[c], psum(job, 4, 64), Zc[:, c], ALU.add), job)
            V(v.tensor_copy(YT[:, :, 0:CH], Y0[:, :, 0:CH]))
            for c in range(1, NCH):
                job = f"yt{c}"
                take(dve, job)
                V.free(tt(YT[:, :, c * CH:(c + 1) * CH], psum(job, 4, CH), Y0[:, :, c * CH:(c + 1) * CH], ALU.add), job)
            take(dve, "sy")
            V.free(v.tensor_copy(YT[:, :, S:T], psum("sy", 4, NB)), "sy")
            for c in range(4):
                take(dve, f"mu{c}")
                V.free(tt(YT[:, c, :], YT[:, c, :], psum(f"mu{c}", T), ALU.subtract), f"mu{c}")
            for c in range(4):
                after(dve, f"va{c}")
                y = YT[:, c, :]
                V(v.reciprocal(e4w[:, c, :], e4w[:, c, :]))
                V(tt(y, y, e4w[:, c, :], ALU.mult))
                V(v.scalar_tensor_tensor(y, y, parT[:, P_GW + c:P_GW + c + 1], bT[:, c, :], ALU.mult, ALU.add))
                V.ready(tt(y, y, gT_[:, c, :], ALU.mult), "obT", c + 1)
            for d in range(KD):
                merge("mb", 1, d)
                V.ready(tt(mixT[:, d, :], sgT[:, d, :], sgT[:, KD + d, :], ALU.add), "mix", d + 1)
            V(v.memset(brow, 0.0))
            V.ready(v.memset(bdn, 0.0), "brow_zero", 1)
            V(v.memset(h2[:, 2, :], 0.0))
            for t, value in ((lgt, BIG), (selr, 0.0), (gate, 0.0), (posx, 0.0), (sel, 0.0), (selg, 0.0), (yS, 0.0), (thr, 1.0)):
                V(v.memset(t, value))
            V.ready(v.memset(selgT, 0.0), "moe_zero", 1)

            def residual(m):
                n = ROWS[m]
                a = lambda g: acc[:n, m, g * 512:(g + 1) * 512]
                if m == 2:
                    take(dve, "wo2")
                    for j in range(4):
                        ins = tt(a(j % 2), PS[bank["wo2"]][32 * j:32 * j + n, :], a(j % 2), ALU.add)
                        V.free(ins, "wo2") if j == 3 else V(ins)
                else:
                    for g in range(2):
                        take(dve, f"wo{m}{g}")
                        V.free(tt(a(g), psum(f"wo{m}{g}", 512, parts=n), a(g), ALU.add), f"wo{m}{g}")

            def norm2(i):
                m = MORDER[i]
                n = ROWS[m]
                dve.wait_ge(S_("rms2"), i + 1)
                V(v.reciprocal(rs1[:n, m:m + 1], rs1[:n, m:m + 1]))
                V.ready(v.scalar_tensor_tensor(h2[:n, m, :], acc[:n, m, :], rs1[:n, m:m + 1], ln2b[:n], ALU.mult, ALU.mult),
                        "h2", i + 1)

            def route(i):
                m = MORDER[i]
                n = ROWS[m]
                take(dve, f"ro{m}")
                V.free(tt(lgt[:n, m, 0:NE], psum(f"ro{m}", NE, parts=n), brow_r[:n], ALU.add), f"ro{m}")
                V(v.max(max8[:n, m, :], lgt[:n, m, :]))
                V(v.match_replace(rep[:n, m, :], max8[:n, m, :], lgt[:n, m, :], NEG))
                V(v.tensor_scalar(ngm[:n, m:m + 1], max8[:n, m, 4:5], -1.0, None, ALU.mult))
                V.ready(v.tensor_scalar(selr[:n, m, :], rep[:n, m, 0:NE], NEG, None, ALU.is_equal), "sel_r", i + 1)

            dve.wait_ge(S_("ld_acc"), 48)
            residual(2)
            residual(0)
            dve.wait_ge(S_("ld_ln"), 32)
            norm2(0)
            norm2(1)
            residual(1)
            dve.wait_ge(S_("ld_router"), 32)
            route(0)
            norm2(2)
            route(1)
            route(2)
            take(dve, "rk")
            for m in range(NM):
                V(v.scalar_tensor_tensor(posx[:, m, 0:NE], psum("rk", 4, NE)[:, m, :], 1.0, selr[:, m, :], ALU.add, ALU.mult))
            for m in range(NM):
                ins = v.tensor_scalar(sel[:ROWS[m], m, :], C["slots"][:ROWS[m], 0:SLOT], posx[:ROWS[m], m, 0:1], None, ALU.is_equal)
                V.ready(ins, "sel", 1) if m == 2 else V(ins)
            V.free(v.tensor_reduce(mcount, psum("rk", 4, NE)[:, 3, :], AX.X, ALU.max), "rk")
            for b in range(1, PASSES):
                V(v.tensor_scalar(thr[:, b:b + 1], mcount, float(SLOT * b), None, ALU.is_gt))
            V(v.tensor_reduce(mcount, thr, AX.X, ALU.add))
            V.ready(v.tensor_copy(npass[:, :], mcount), "npass", 1)
            dve.wait_ge(S_("r_exp"), 3)
            for m in range(NM):
                n = ROWS[m]
                V(tt(gate[:n, m, :], rexp[:n, m, :], selr[:n, m, :], ALU.mult))
                V(v.tensor_reduce(gsum[:n, m:m + 1], gate[:n, m, :], AX.X, ALU.add))
                V(v.reciprocal(gsum[:n, m:m + 1], gsum[:n, m:m + 1]))
                V.ready(v.tensor_scalar(gate[:n, m, :], gate[:n, m, :], gsum[:n, m:m + 1], None, ALU.mult), "gate", m + 1)
            for b in range(1, PASSES):
                V(v.tensor_scalar(posx[:, :, b * NE:(b + 1) * NE], posx[:, :, 0:NE], float(-SLOT * b), None, ALU.add))
            passes = dve.value_load(npass[0:1, 0:1], min_val=1, max_val=PASSES)
            V(v.memset(mcount, 0.0))
            dve.sem_inc(S_("acc_done"), 2)
            dve.wait_ge(S_("acc_done"), 2)

            def accumulate(it, m):
                n = ROWS[m]
                dve.wait_ge(S_("cmb_full"), it * 3 + (m + 1))
                for g in range(2):
                    a = acc[:n, m, g * 512:(g + 1) * 512]
                    tt(a, PS[CMB[m][g]][:n, :], a, ALU.add).then_inc(S_("acc_done"), 1)

            with dve.Fori(0, passes) as p:
                with dve.Fori(0, NE) as ex:
                    it = dve.snap(p * NE + ex)
                    dve.wait_ge(S_("unit_used"), it * 12 + 20)
                    v.tensor_scalar(gt, PS[2][:, :], LIMIT, None, ALU.min).then_inc(S_("gt"), 1)
                    v.tensor_scalar(up, PS[3][:, :], LIMIT, -LIMIT, ALU.min, ALU.max).then_inc(S_("up"), 1)
                    for m in range(NM):
                        n = ROWS[m]
                        v.tensor_scalar(sel[:n, m, :], C["slots"][:n, 0:SLOT], posx[:n, m, bass.ds(it + 1, 1)], None,
                                        ALU.is_equal).then_inc(S_("sel_next"), 1)
                    dve.wait_ge(S_("gt"), it + 1)
                    dve.wait_ge(S_("up"), it + 1)
                    v.scalar_tensor_tensor(up, up, 1.0, gt, ALU.add, ALU.mult).then_inc(S_("upgt"), 1)
                    dve.wait_ge(S_("upgt"), it + 1)
                    dve.wait_ge(S_("sg"), it + 1)
                    tt(up, up, sg, ALU.mult).then_inc(S_("act"), 1)
                    dve.wait_ge(S_("acc_done"), it * 6 + 2)
                    accumulate(it, 0)
                    for m in range(NM):
                        n = ROWS[m]
                        v.tensor_scalar(selg[:n, m, :], C["slots"][:n], posx[:n, m, bass.ds(it, 1)],
                                        gate[:n, m, bass.ds(ex, 1)], ALU.is_equal, ALU.mult).then_inc(S_("selg"), 1)
                    accumulate(it, 1)
                    accumulate(it, 2)
            last = dve.snap(passes * NE)
            dve.wait_ge(S_("acc_done"), last * 6 + 2)
            for m in range(NM):
                accumulate(last, m)
            for m in range(NM):
                n = ROWS[m]
                dve.wait_ge(S_("rms3"), m + 1)
                V(v.reciprocal(rs1[:n, m:m + 1], rs1[:n, m:m + 1]))
                v.scalar_tensor_tensor(acc[:n, m, :], acc[:n, m, :], rs1[:n, m:m + 1], lnfb[:n], ALU.mult, ALU.mult)\
                 .then_inc(S_("y"), 1)

        @block.tensor
        def _(pe):
            mm = nc.tensor.matmul

            def give(job):
                if turn[job] > 1:
                    pe.wait_ge(evac[bank[job]], turn[job] - 1)

            def done(ins, job):
                ins.then_inc(full[bank[job]], 1)

            def transposes(job, pieces, width, parts=128):
                give(job)
                for n, src in enumerate(pieces):
                    rows = src.shape[0]
                    last = nc.tensor.transpose(PS[bank[job]][:parts, n * width:n * width + rows], src, C["ident"][:rows, :rows])
                done(last, job)

            pe.wait_ge(S_("ld_ident"), 16)
            pe.wait_ge(S_("ld_par"), 16 * 9)
            transposes("par", [par[:P_N, :]], P_N)
            pe.wait_ge(S_("ld_ss"), 16)
            transposes("ssT", [ss[:NB, c * 128:(c + 1) * 128] for c in range(CR)], NB)
            for m in range(NM):
                pe.wait_ge(S_("xs"), m + 1)
                for g in range(2):
                    transposes(f"hT{m}{g}", [XS[:ROWS[m], m, (4 * g + c) * 128:(4 * g + c + 1) * 128] for c in range(4)], ROWS[m])
            after(pe, "hT20", "hT21")
            def project(*groups):
                for g in groups:
                    gi = GROUPS.index(g)
                    for j in range(GC):
                        if gi and j == 0:
                            pe.wait_ge(S_(f"ld_win{gi}"), 16)
                        elif gi == 0 and j % 3 == 0:
                            pe.wait_ge(S_("ld_win0" + "ab"[j // 3]), 16)
                        job = f"pr{g * GC + j}"
                        give(job)
                        for k in range(KD):
                            last = mm(psum(job, T), WIN[gi % 2][:, k, j * 128:(j + 1) * 128], hT[:, k, :], start=k == 0, stop=k == KD - 1)
                        done(last, job)

            project(2, 3, 4)
            pe.wait_ge(S_("ld_mats"), 16)
            pe.wait_ge(S_("relb64"), 1)
            give("bvp")
            done(mm(psum("bvp", NREL, parts=H), relb[:32, :], hot_p[:32], start=True, stop=True), "bvp")
            give("bvs")
            done(mm(psum("bvs", NKEY, parts=64), relb64[:32].rearrange("p a b -> p (a b)"), hot_s[:32], start=True, stop=True), "bvs")
            for g in range(4):
                transposes(f"sh{g}", [rcT[:, c, S - 1:T] for c in range(4 * g, min(4 * g + 4, CR))], 128, NB + 1)
            project(0)
            pe.wait_ge(S_("ld_lora"), 48)
            pe.wait_ge(S_("lora_in"), 2)
            for k, lo, hi, w, src in (("lw", 0, 64, 0, 12), ("la", 64, 128, 0, 12), ("lg", 0, 128, 1, 13)):
                for c in range(4):
                    give(f"{k}{c}")
                    done(mm(psum(f"{k}{c}", T), wlora[lo:hi, w, c * 128:(c + 1) * 128], xr[lo:hi, src, :], start=True, stop=True), f"{k}{c}")
            project(1)
            pe.wait_ge(S_("kk_sq"), 1)
            for c in range(4):
                give(f"nk{c}")
                done(mm(psum(f"nk{c}", T), C["head_sum"], bT[:, c, :], start=True, stop=True), f"nk{c}")
            def natural(name, at):
                for m in range(NM):
                    transposes(f"{name}{m}", [qkvT[:, at + c, m * 128:m * 128 + ROWS[m]] for c in range(4)], 128, ROWS[m])

            transposes("qn", [qkvT[:, c, S:T] for c in range(4)], 128, NB)
            natural("kn", 4)
            project(5)
            project(6)
            natural("vn", 8)
            def score(h):
                q = slice((h % 2) * 64, (h % 2) * 64 + 64)
                give(f"s{h}")
                w = psum(f"s{h}", 384)
                mm(w[:, 0:128], qkvT[q, h // 2, 0:128], qkvT[q, 4 + h // 2, 0:128], start=True, stop=True)
                done(mm(w[:, 128:384], qkvT[q, h // 2, 128:256], qkvT[q, 4 + h // 2, 0:256], start=True, stop=True), f"s{h}")
            score(0)
            score(1)

            def decode(g):
                if g == 0:
                    after(pe, "spt")
                for j in range(4):
                    pe.wait_ge(S_(f"ld_v{4 * g + j}"), 64)
                job = f"pv{g}"
                give(job)
                for t in range(3):
                    for j in range(4):
                        last = mm(psum(job, 512)[32 * j:32 * j + 32], pts[:KT[t], t, 4 * g + j, :], Vb[4 * g + j][:KT[t], t, :],
                                  start=t == 0, stop=t == 2)
                done(last, job)

            for h in range(H):
                if h + 2 < H:
                    score(h + 2)
                pe.wait_ge(S_("pn"), h + 1)
                transposes(f"pt{h}", [ssb[:, h % 2, 128 * t:128 * t + 128] for t in range(3)], 128)
                if h % 2:
                    job = f"ov{h // 2}"
                    give(job)
                    for hh in (h - 1, h):
                        after(pe, f"pt{hh}")
                        q = slice((hh % 2) * 64, (hh % 2) * 64 + 64)
                        mm(psum(job, S)[q, :], vn[:, 0, hh * 64:hh * 64 + 64], ptb[:, hh % 2, 0:256], start=True, stop=False)
                        last = mm(psum(job, S)[q, 128:256], vn[:, 1, hh * 64:hh * 64 + 64], ptb[:, hh % 2, 256:384], start=False, stop=True)
                    done(last, job)
                if h == 0:
                    pe.wait_ge(S_("rk"), 1)
                if h < 6:
                    transposes(f"sx{h}", [svT[:, h, c, :] for c in range(4)], 128, NB)
                if h >= 4:
                    job = f"bo{h - 4}"
                    give(job)
                    done(mm(psum(job, T), C["head_sum"], bT[:, h - 4, :], start=True, stop=True), job)
                if h == 3:
                    pe.wait_ge(S_("s_red"), NB)
                    give("sst")
                    for t in range(3):
                        last = nc.tensor.transpose(PS[bank["sst"]][:64, KO[t]:KO[t] + KT[t]], scs[:KT[t], t, :], C["ident"][:KT[t], :KT[t]])
                    done(last, "sst")
                if h == 6:
                    pe.wait_ge(S_("s_pn"), 1)
                    give("spt")
                    for t in range(3):
                        last = nc.tensor.transpose(PS[bank["spt"]][:KT[t], t * 64:t * 64 + 64], s64[:64, KO[t]:KO[t] + KT[t]], C["ident"][:64, :64])
                    done(last, "spt")
                if h == 7:
                    decode(0)
            decode(1)
            after(pe, "pv0", "pv1")
            give("sv")
            for c in range(4):
                for g in range(2):
                    last = mm(psum("sv", 4, 2, 4)[:, c, g, :], pvm[:, g, c * 128:(c + 1) * 128], C["quad"][:, 0:4], start=True, stop=True)
            done(last, "sv")
            for m in range(2):
                tok = slice(m * 128, m * 128 + 128)
                transposes(f"tV{m}", [xr[:, 8 + c, tok] for c in range(4)], 128)
                transposes(f"tK{m}", [e[1][:, c, tok] for c in range(4)], 128)
                transposes(f"tC{m}", [e[4][:, c, tok] for c in range(4)], 128)
                transposes(f"tB{m}", [e[3][:, c, tok] for c in range(4)], 128)

            def heads(kind, fn, *waits):
                for g, (m, pr) in enumerate(GRP):
                    job = f"{kind}{m}{pr}"
                    for w in waits:
                        after(pe, f"{w}{m}{pr}")
                    if kind == "X1T":
                        pe.wait_ge(S_("imat"), g + 1)
                    give(job)
                    for hh in range(4):
                        last = fn(psum(job, 4, 128)[:, hh, :], g, m, pr, hh)
                    done(last, job)

            def pairs(lhs, rhs):
                def fn(out, g, m, pr, hh):
                    q = slice(pr * 64, pr * 64 + 64)
                    tok = slice(m * 128, m * 128 + 128)
                    return mm(out, lhs[q, hh, tok], rhs[q, hh, tok], start=True, stop=True)
                return fn

            def prod(lhs, rhs):
                return lambda out, g, m, pr, hh: mm(out, lhs[:, g, hh, :], rhs[:, g, hh, :], start=True, stop=True)

            rt, kt, bbar, kbar = e[0], e[1], e[2], e[5]
            heads("Auk", pairs(kbar, kt))
            heads("Brk", pairs(kbar, rt))
            heads("Aub", pairs(bbar, kt))
            heads("Brb", pairs(bbar, rt))
            heads("A8", pairs(kt, bbar))
            heads("A2", prod(aAT, aA), "A8", "Aub")
            heads("A2T", prod(aA, aAT))
            heads("X1T", prod(aI, aAT), "A2")
            heads("A4", prod(aA2T, aA2), "A2T")
            heads("X", prod(aA, aI), "X1T", "A4")
            heads("XT", prod(aI, aA))
            heads("LX", prod(aL1T, aA2), "X")
            heads("X2", prod(aA2T, aAT), "LX", "XT")
            heads("X2T", prod(aAT, aA2T))
            heads("LX2", prod(aL2T, aA), "X2")
            heads("MT", prod(aA2, aI), "LX2", "X2T")
            after(pe, "tV1", "tK1", "tC1", "tB1")
            head = lambda pr, hh: slice((2 * hh + pr) * 64, (2 * hh + pr) * 64 + 64)
            for g, (m, pr) in enumerate(GRP):
                job = f"AV{m}{pr}"
                give(job)
                for hh in range(4):
                    last = mm(psum(job, 4, 64)[:, hh, :], aAuk[:, g, hh, :], natV[:, m, head(pr, hh)], start=True, stop=True)
                done(last, job)

            def hg(out, g, m, pr, hh):
                a, b = AV[:, g, hh, :], natK[:, m, head(pr, hh)]
                both = bass.AP(a.tensor, a.offset, [list(a.ap[0]), [b.offset - a.offset, 2], [1, 64]])
                return mm(out, aA2T[:, g, hh, :], both, start=True, stop=True)

            def y0(out, g, m, pr, hh):
                q = slice(pr * 64, pr * 64 + 64)
                mm(out[q], natV[:, m, head(pr, hh)], aBrk[:, g, hh, :], start=True, stop=False)
                return mm(out[q], HG[:, g, hh, 0:64], aBrb[:, g, hh, :], start=False, stop=True)

            def rp(out, g, m, pr, hh):
                q = slice(pr * 64, pr * 64 + 64)
                return mm(out[q], HG[:, g, hh, 64:128], aBrb[:, g, hh, :], start=True, stop=True)

            heads("HG", hg, "MT", "AV")
            heads("Y0", y0, "HG")
            heads("Rp", rp)
            def transfer(m):
                chunks = range(4 * m, 4 * m + 4)
                for c in chunks:
                    give(f"TZ{c}")
                for h in range(H):
                    pr, hh = h % 2, h // 2
                    g, q, hs = m * 2 + pr, slice(pr * 64, pr * 64 + 64), head(pr, hh)
                    for c in chunks:
                        r = slice((c % 4) * CH, (c % 4) * CH + CH)
                        if c:
                            mm(psum(f"TZ{c}", 2, 4, 64)[q, 0, hh, :], HG[r, g, hh, 64:128], natB[r, m, hs], start=True, stop=True)
                    for c in chunks:
                        r = slice((c % 4) * CH, (c % 4) * CH + CH)
                        mm(psum(f"TZ{c}", 2, 4, 64)[q, 1, hh, :], natC[r, m, hs], natV[r, m, hs], start=True, stop=False)
                    for c in chunks:
                        r = slice((c % 4) * CH, (c % 4) * CH + CH)
                        last = mm(psum(f"TZ{c}", 2, 4, 64)[q, 1, hh, :], natB[r, m, hs], HG[r, g, hh, 0:64], start=False, stop=True)
                        if h == H - 1:
                            done(last, f"TZ{c}")

            def branch(k, d, w, src):
                give(f"{k}{d}")
                for c in range(4):
                    last = mm(psum(f"{k}{d}", T), w[:, c, d * 128:(d + 1) * 128], src[:, c, :], start=c == 0, stop=c == 3)
                done(last, f"{k}{d}")

            def state(c):
                after(pe, f"TZ{c}")
                after(pe, f"st{c - 1}") if c > 1 else pe.wait_ge(S_("state"), 1)
                give(f"st{c}")
                for hh in range(4):
                    last = mm(psum(f"st{c}", 4, 64)[:, hh, :], TT[:, c, hh, :], stc[c - 1][:, hh, :], start=True, stop=True)
                done(last, f"st{c}")

            for job in STATE_JOBS:
                c = int(job[2:])
                if job in ("TZ0", "TZ4"):
                    transfer(c // 4)
                elif job[:2] == "st":
                    state(c)
                elif job[:2] == "ma":
                    if c == 0:
                        pe.wait_ge(S_("ld_wa"), 16)
                    branch("ma", c, wa, oaT)
            after(pe, "Rp10", "Rp11")
            for c in range(1, NCH):
                job = f"yt{c}"
                pe.wait_ge(S_("std"), c)
                give(job)
                d = STd[:, c - 1] if c - 1 < 4 else STe[:, c - 5]
                for hh in range(4):
                    last = mm(psum(job, 4, CH)[:, hh, :], d[:, hh, :], Rp[:, hh, c * CH:(c + 1) * CH], start=True, stop=True)
                done(last, job)
            after(pe, f"st{NCH - 1}")
            transposes("wkv", [stc[NCH - 1][:, hh, :] for hh in range(4)], 128, 64)
            pe.wait_ge(S_("ld_ysn"), 16)
            transposes("sy", [ysn[:NB, c * 128:(c + 1) * 128] for c in range(4)], NB)
            after(pe, "wkv", "sy")
            pe.sem_inc(S_("unit_used"), 4)
            for c in range(4):
                give(f"mu{c}")
                done(mm(psum(f"mu{c}", T), C["head_mean"], YT[:, c, :], start=True, stop=True), f"mu{c}")
            for c in range(4):
                pe.wait_ge(S_("y_sq"), c + 1)
                give(f"va{c}")
                done(mm(psum(f"va{c}", T), C["head_mean"], e4w[:, c, :], start=True, stop=True), f"va{c}")
            pe.wait_ge(S_("ld_wb"), 16)
            for c in range(4):
                pe.wait_ge(S_("obT"), c + 1)
                for d in range(KD):
                    if c == 0:
                        give(f"mb{d}")
                    last = mm(psum(f"mb{d}", T), wb[:, c, d * 128:(d + 1) * 128], YT[:, c, :], start=c == 0, stop=c == 3)
                    if c == 3:
                        done(last, f"mb{d}")
            pe.wait_ge(S_("ld_wo"), 16)

            def out_projection(m, g):
                job = f"wo{m}{g}"
                give(job)
                for k in range(KD):
                    last = mm(psum(job, 512), mixT[:, k, m * 128:m * 128 + 128],
                              wo[:, k, g * 512:(g + 1) * 512], start=k == 0, stop=k == KD - 1)
                done(last, job)

            def h2_T(i):
                m = MORDER[i]
                pe.wait_ge(S_("h2"), i + 1)
                for g in range(2):
                    transposes(f"ht{m}{g}", [h2[:ROWS[m], m, (4 * g + c) * 128:(4 * g + c + 1) * 128] for c in range(4)], ROWS[m])

            def logits(m):
                n = ROWS[m]
                after(pe, f"ht{m}0", f"ht{m}1")
                give(f"ro{m}")
                for k in range(KD):
                    last = mm(psum(f"ro{m}", NE, parts=n), h2T[:, k, m * 128:m * 128 + n], wr[:, k, :], start=k == 0, stop=k == KD - 1)
                done(last, f"ro{m}")

            give("wo2")
            for k in range(4):
                pe.wait_ge(S_("mix"), 2 * k + 2)
                for j in range(4):
                    kk, g = 2 * k + j // 2, j % 2
                    last = mm(PS[bank["wo2"]][32 * j:32 * j + NB, :], mixT[:, kk, S:T], wo[:, kk, g * 512:(g + 1) * 512],
                              start=k == 0, stop=k == 3)
            done(last, "wo2")
            after(pe, "ma7", "mb7")
            pe.sem_inc(S_("unit_used"), 4)
            for g in range(2):
                out_projection(0, g)
            h2_T(0)
            out_projection(1, 0)
            h2_T(1)
            out_projection(1, 1)
            pe.wait_ge(S_("ld_router"), 32)
            logits(2)
            logits(0)
            after(pe, "wo10", "wo11")
            pe.sem_inc(S_("unit_used"), 4)
            h2_T(2)
            logits(1)
            give("rk")
            rk = psum("rk", 4, NE)
            for i, m in enumerate(MORDER):
                pe.wait_ge(S_("sel_r"), i + 1)
                mm(rk[:, m, :], C["before"], selr[:, m, :], start=i == 0, stop=False)
                for later in MORDER[i + 1:]:
                    mm(rk[:, later, :], C["ones"], selr[:, m, :], start=False, stop=False)
                last = mm(rk[:, 3, :], C["ones"], selr[:, m, :], start=False, stop=i == 2)
            done(last, "rk")

            def gather(it, sem_name, count):
                pe.wait_ge(S_(sem_name), count)
                for m in range(NM):
                    for g in range(2):
                        last = mm(PS[0][g * 64:g * 64 + 64, :], sel[:, m, :], h2[:, m, g * 512:(g + 1) * 512],
                                  start=m == 0, stop=m == NM - 1)
                last.then_inc(S_("xg_full"), 1)

            def gather_T(it):
                pe.wait_ge(S_("xg_out"), it + 1)
                for c in range(4):
                    last = nc.tensor.transpose(PS[1][:, c * 128:(c + 1) * 128], xg[:, c * 128:(c + 1) * 128], C["ident"])
                last.then_inc(S_("xgT_full"), 1)

            def bank_free(b):
                pe.wait_ge(evac[b], max(turn[j] for j in jobs if bank[j] == b))

            bank_free(0)
            bank_free(1)
            gather(0, "sel", 1)
            gather_T(0)
            for b in range(2, 8):
                bank_free(b)

            def combine(it):
                pe.wait_ge(S_("selgT_out"), it + 1)
                pe.wait_ge(S_("y_out"), it + 1)
                pe.wait_ge(S_("acc_done"), it * 6 + 2)
                for m in range(NM):
                    for g in range(2):
                        q = slice(g * 64, g * 64 + 64)
                        last = mm(PS[CMB[m][g]][:, :], selgT[q, m * 128:(m + 1) * 128], yS[q, :], start=True, stop=True)
                    last.then_inc(S_("cmb_full"), 1)

            pe.wait_ge(S_("npass"), 1)
            pe.wait_ge(S_("moe_zero"), 1)
            passes = pe.value_load(npass[0:1, 0:1], min_val=1, max_val=PASSES)
            with pe.Fori(0, passes) as p:
                with pe.Fori(0, NE) as ex:
                    it = pe.snap(p * NE + ex)
                    pe.wait_ge(S_("ld_b"), it * 16 + 16)
                    for bnk, base in ((2, 0), (3, 1024)):
                        for g in range(2):
                            mm(PS[bnk][g * 64:g * 64 + 64, :], C["ones"][:, 0:64],
                               brow[:, base + g * 512:base + (g + 1) * 512], start=True, stop=False)
                    pe.wait_ge(S_("xgT_out"), it + 1)
                    for k in range(KD):
                        pe.wait_ge(S_(f"ld_u{k}"), it * 16 + 16)
                        h_, c_ = k // 4, k % 4
                        lhs = xgT[:, c_, h_ * 64:h_ * 64 + 64]
                        for bnk, base in ((2, 0), (3, 1024)):
                            for g in range(2):
                                last = mm(PS[bnk][g * 64:g * 64 + 64, :], lhs,
                                          UNIT[k][:, base + g * 512:base + (g + 1) * 512], start=False, stop=k == KD - 1)
                        last.then_inc(S_("unit_used"), 1)
                    combine(it)
                    pe.wait_ge(S_("acc_done"), it * 6 + 4)
                    gather(it, "sel_next", it * 3 + 3)
                    pe.wait_ge(S_("selg"), it * 3 + 3)
                    pe.wait_ge(S_("acc_done"), it * 6 + 8)
                    for m in range(NM):
                        last = nc.tensor.transpose(PS[5][:, m * 128:(m + 1) * 128], selg[:, m, :], C["ident"])
                    last.then_inc(S_("selgT_full"), 1)
                    gather_T(it + 1)
                    pe.wait_ge(S_("act"), it + 1)
                    for c in range(4):
                        last = nc.tensor.transpose(PS[4][:, c * 128:(c + 1) * 128], up[:, c * 128:(c + 1) * 128], C["ident"])
                    last.then_inc(S_("actT_full"), 1)
                    pe.wait_ge(S_("ld_bd"), it * 16 + 16)
                    pe.wait_ge(S_("selgT_out"), it + 2)
                    for g in range(2):
                        mm(PS[5][g * 64:g * 64 + 64, :], C["ones"][:, 0:64], bdn[:, g * 512:(g + 1) * 512], start=True, stop=False)
                    pe.wait_ge(S_("actT_out"), it + 1)
                    for k in range(KD):
                        u = KD + k // 2
                        if k % 2 == 0:
                            pe.wait_ge(S_(f"ld_u{u}"), it * 16 + 16)
                        h_, c_ = k // 4, k % 4
                        lhs = actT[:, c_, h_ * 64:h_ * 64 + 64]
                        for g in range(2):
                            w0 = (k % 2) * 1024 + g * 512
                            last = mm(PS[5][g * 64:g * 64 + 64, :], lhs, UNIT[u][:, w0:w0 + 512], start=False, stop=k == KD - 1)
                        if k % 2:
                            last.then_inc(S_("unit_used"), 1)
            combine(pe.snap(passes * NE))


_INS = ["x_prompt", "x_sample", "cache_k", "cache_v", "state_wkv", "state_shift", "rel_bias", "ln1", "w_in", "rwkv_mu",
        "w0", "w_decay_up", "a0", "w_a_up", "w_g_up", "k_k", "k_a", "r_k", "gn_w", "gn_b", "w_branch_a", "w_branch_b",
        "w_out", "ln2", "w_router", "b_router", "w_gate_up", "b_gate_up", "w_down", "b_down", "ln_f"]
_OUTS = [("yp", (1, S, D)), ("ys", (NB, 1, D)), ("pk", (1, 1, S, H, E64)), ("pv", (1, 1, S, H, E64)),
         ("pwkv", (1, 1, H, E64, E64)), ("pshift", (1, 1, RC)), ("sk", (1, NB, 1, H, E64)), ("sv", (1, NB, 1, H, E64)),
         ("swkv", (1, NB, H, E64, E64)), ("sshift", (1, NB, RC))]


def kernel(**inputs):
    import concourse.bacc as bacc
    from concourse.bass_utils import run_bass_kernel_spmd

    nc = bacc.Bacc("TRN2", target_bir_lowering=False, num_devices=1)
    arrays = {f"in_{n}": np.ascontiguousarray(inputs[n]) for n in _INS}
    arrays.update({f"in_{n}": a for n, a in shape_constants().items()})
    A = {n[3:]: nc.dram_tensor(n, a.shape, mybir.dt.from_np(a.dtype), kind="ExternalInput").ap() for n, a in arrays.items()}
    O = {n: nc.dram_tensor(f"out_{n}", shape, F32, kind="ExternalOutput").ap() for n, shape in _OUTS}
    build(nc, A, O)
    r = run_bass_kernel_spmd(nc, [arrays], core_ids=[0])
    return tuple(r.results[0][f"out_{n}"] for n, _ in _OUTS)
```
